# Optimizing a Trainium2 kernel written in Bass

```python
import jax, jax.numpy as jnp
from jax import lax
import numpy as np

D_MODEL = 1024
BATCH = 1
SEQ = 512
DEPTH = 1

D_PLE = 256
D_MIX = 2 * D_MODEL
GM_WIDTH = D_MIX // 2
GM_HEADS = 8
GM_HEAD_DIM = GM_WIDTH // GM_HEADS
GM_CHUNK = 128
SSD_WIDTH = D_MIX - GM_WIDTH
SSD_HEAD_DIM = 64
SSD_HEADS = SSD_WIDTH // SSD_HEAD_DIM
SSD_GROUPS = 2
SSD_HEADS_PER_GROUP = SSD_HEADS // SSD_GROUPS
SSD_STATE = 128
SSD_CONV = 4
SSD_CHUNK = 128
D_FF = 4 * D_MODEL
EPS = 1e-6
GM_COLS = 2 * GM_WIDTH
SSD_CONV_CH = SSD_WIDTH + 2 * SSD_GROUPS * SSD_STATE
SSD_COLS = SSD_WIDTH + SSD_CONV_CH + SSD_HEADS
D_IN_PROJ = GM_COLS + SSD_COLS

kernel_name = "hybrid_gmlp_ssd_parallel_heads"

def rmsnorm(x, g):
    xf = x.astype(jnp.float32)
    y = xf * lax.rsqrt(jnp.mean(xf * xf, axis=-1, keepdims=True) + EPS)
    return (y * g.astype(jnp.float32)).astype(x.dtype)

def gmlp_chunk_mixer(uv, v_norm_g, ws, bs, out_norm_g):
    b, s, _ = uv.shape
    nc = s // GM_CHUNK
    uv = jax.nn.gelu(uv, approximate=False)
    u = uv[..., :GM_WIDTH].reshape(b, nc, GM_CHUNK, GM_HEADS, GM_HEAD_DIM)
    v = uv[..., GM_WIDTH:].reshape(b, s, GM_HEADS, GM_HEAD_DIM)
    v = rmsnorm(v, v_norm_g.reshape(GM_HEADS, GM_HEAD_DIM))
    v = v.reshape(b, nc, GM_CHUNK, GM_HEADS, GM_HEAD_DIM)
    causal = jnp.tril(jnp.ones((GM_CHUNK, GM_CHUNK), dtype=bool))
    w = jnp.where(causal[None], ws, jnp.zeros_like(ws))
    mixed = jnp.einsum('hts,bcshp->bcthp', w, v) + bs.T[None, None, :, :, None]
    y = (u * mixed).reshape(b, s, GM_WIDTH)
    return rmsnorm(y, out_norm_g)

def causal_depthwise_conv(x, w, bias):
    out = lax.conv_general_dilated(
        x, w[:, None, :], window_strides=(1,), padding=[(SSD_CONV - 1, 0)],
        dimension_numbers=('NWC', 'WIO', 'NWC'), feature_group_count=x.shape[-1])
    return out + bias

def ssd_chunked_scan(x, dt, A, B, C):
    b, s, G, R, P = x.shape
    N = B.shape[-1]
    nc, L = s // SSD_CHUNK, SSD_CHUNK
    x = x.reshape(b, nc, L, G, R, P)
    dt = dt.reshape(b, nc, L, G, R)
    B = B.reshape(b, nc, L, G, N)
    C = C.reshape(b, nc, L, G, N)
    cs = jnp.cumsum(dt * A, axis=2)
    x_dt = x * dt[..., None].astype(x.dtype)
    seg = cs[:, :, :, None] - cs[:, :, None, :]
    causal = jnp.tril(jnp.ones((L, L), dtype=bool))[:, :, None, None]
    lmat = jnp.exp(jnp.where(causal, seg, -jnp.inf)).astype(x.dtype)
    cb = jnp.einsum('bclgn,bcsgn->bclsg', C, B)
    y_diag = jnp.einsum('bclsgr,bcsgrp->bclgrp', cb[..., None] * lmat, x_dt)
    decay_states = jnp.exp(cs[:, :, -1:] - cs).astype(x.dtype)
    states = jnp.einsum('bclgn,bclgr,bclgrp->bcgrpn', B, decay_states, x_dt)
    chunk_decay = jnp.exp(cs[:, :, -1]).astype(x.dtype)

    def step(carry, inp):
        st, dec = inp
        return carry * dec[..., None, None] + st, carry

    init = jnp.zeros((b, G, R, P, N), dtype=states.dtype)
    _, prev = lax.scan(step, init, (jnp.moveaxis(states, 1, 0), jnp.moveaxis(chunk_decay, 1, 0)))
    prev = jnp.moveaxis(prev, 0, 1)
    y_off = jnp.einsum('bclgn,bcgrpn,bclgr->bclgrp', C, prev, jnp.exp(cs).astype(x.dtype))
    return (y_diag + y_off).reshape(b, s, G, R, P)

def ssd_mixer(zxbcdt, conv_w, conv_b, dt_bias, a_log, d_skip, norm_g):
    b, s, _ = zxbcdt.shape
    z = zxbcdt[..., :SSD_WIDTH]
    xbc = zxbcdt[..., SSD_WIDTH:SSD_WIDTH + SSD_CONV_CH]
    dt_raw = zxbcdt[..., SSD_WIDTH + SSD_CONV_CH:]
    xbc = jax.nn.silu(causal_depthwise_conv(xbc, conv_w, conv_b))
    xs = xbc[..., :SSD_WIDTH].reshape(b, s, SSD_GROUPS, SSD_HEADS_PER_GROUP, SSD_HEAD_DIM)
    Bm = xbc[..., SSD_WIDTH:SSD_WIDTH + SSD_GROUPS * SSD_STATE].reshape(b, s, SSD_GROUPS, SSD_STATE)
    Cm = xbc[..., SSD_WIDTH + SSD_GROUPS * SSD_STATE:].reshape(b, s, SSD_GROUPS, SSD_STATE)
    dt = jax.nn.softplus(dt_raw.astype(jnp.float32) + dt_bias.astype(jnp.float32))
    dt = dt.reshape(b, s, SSD_GROUPS, SSD_HEADS_PER_GROUP)
    A = -jnp.exp(a_log.astype(jnp.float32)).reshape(SSD_GROUPS, SSD_HEADS_PER_GROUP)
    y = ssd_chunked_scan(xs, dt, A, Bm, Cm)
    y = y + d_skip.reshape(SSD_GROUPS, SSD_HEADS_PER_GROUP)[:, :, None] * xs
    y = y.reshape(b, s, SSD_WIDTH) * jax.nn.silu(z)
    gw = SSD_WIDTH // SSD_GROUPS
    y = rmsnorm(y.reshape(b, s, SSD_GROUPS, gw), norm_g.reshape(SSD_GROUPS, gw))
    return y.reshape(b, s, SSD_WIDTH)

def setup_inputs(seed: int = 0) -> dict:
    key = jax.random.key(seed)
    ks = jax.random.split(key, 24)
    f32 = jnp.float32
    nrm = lambda k, shape, scale: jax.random.normal(k, shape, f32) * scale
    gain = lambda k, shape: 1.0 + 0.05 * jax.random.normal(k, shape, f32)
    dt_init = jnp.exp(jax.random.uniform(ks[14], (DEPTH, SSD_HEADS), f32,
                                         np.log(1e-3).astype(np.float32), np.log(1e-1).astype(np.float32)))
    return {
        "x": jax.random.normal(ks[0], (BATCH, SEQ, D_MODEL), f32),
        "p": jax.random.normal(ks[1], (DEPTH, BATCH, SEQ, D_PLE), f32),
        "norm_mix_g": gain(ks[2], (DEPTH, D_MODEL)),
        "w_in": nrm(ks[3], (DEPTH, D_MODEL, D_IN_PROJ), D_MODEL ** -0.5),
        "gm_v_norm_g": gain(ks[4], (DEPTH, GM_WIDTH)),
        "gm_ws": nrm(ks[5], (DEPTH, GM_HEADS, GM_CHUNK, GM_CHUNK), GM_CHUNK ** -0.5),
        "gm_bs": gain(ks[6], (DEPTH, GM_HEADS, GM_CHUNK)),
        "gm_out_norm_g": gain(ks[7], (DEPTH, GM_WIDTH)),
        "ssd_conv_w": nrm(ks[8], (DEPTH, SSD_CONV, SSD_CONV_CH), SSD_CONV ** -0.5),
        "ssd_conv_b": nrm(ks[9], (DEPTH, SSD_CONV_CH), 0.02),
        "ssd_dt_bias": dt_init + jnp.log(-jnp.expm1(-dt_init)),
        "ssd_a_log": jnp.log(jax.random.uniform(ks[10], (DEPTH, SSD_HEADS), f32, 1.0, 16.0)),
        "ssd_d": gain(ks[11], (DEPTH, SSD_HEADS)),
        "ssd_norm_g": gain(ks[12], (DEPTH, SSD_WIDTH)),
        "w_out": nrm(ks[13], (DEPTH, D_MIX, D_MODEL), D_MIX ** -0.5),
        "norm_mlp_g": gain(ks[15], (DEPTH, D_MODEL)),
        "w_ff1": nrm(ks[16], (DEPTH, D_MODEL, D_FF), D_MODEL ** -0.5),
        "w_ff2": nrm(ks[17], (DEPTH, D_FF, D_MODEL), D_FF ** -0.5),
        "ple_norm_g": gain(ks[18], (DEPTH, D_MODEL)),
        "w_ple_gate": nrm(ks[19], (DEPTH, D_MODEL, D_MODEL), D_MODEL ** -0.5),
        "w_ple_proj": nrm(ks[20], (DEPTH, D_PLE, D_MODEL), D_PLE ** -0.5),
        "final_norm_g": gain(ks[21], (D_MODEL,)),
    }

def reference(x, p, norm_mix_g, w_in, gm_v_norm_g, gm_ws, gm_bs, gm_out_norm_g,
              ssd_conv_w, ssd_conv_b, ssd_dt_bias, ssd_a_log, ssd_d, ssd_norm_g,
              w_out, norm_mlp_g, w_ff1, w_ff2, ple_norm_g, w_ple_gate, w_ple_proj,
              final_norm_g):
    h = x
    for i in range(DEPTH):
        proj = rmsnorm(h, norm_mix_g[i]) @ w_in[i]
        y_a = gmlp_chunk_mixer(proj[..., :GM_COLS], gm_v_norm_g[i], gm_ws[i], gm_bs[i],
                               gm_out_norm_g[i])
        y_b = ssd_mixer(proj[..., GM_COLS:], ssd_conv_w[i], ssd_conv_b[i], ssd_dt_bias[i],
                        ssd_a_log[i], ssd_d[i], ssd_norm_g[i])
        h = h + jnp.concatenate([y_a, y_b], axis=-1) @ w_out[i]
        hid = jax.nn.relu(rmsnorm(h, norm_mlp_g[i]) @ w_ff1[i])
        h = h + (hid * hid) @ w_ff2[i]
        gate = jax.nn.sigmoid(rmsnorm(h, ple_norm_g[i]) @ w_ple_gate[i])
        h = h + gate * (p[i] @ w_ple_proj[i])
    return rmsnorm(h, final_norm_g)


_drawn_inputs = setup_inputs


def setup_inputs(seed=0):
    import zlib

    import numpy as np

    out = dict(_drawn_inputs(seed))
    spreads = {}
    factors = {'gm_v_norm_g': 4.006, 'ssd_conv_b': 3.87, 'ple_norm_g': 25.791, 'gm_bs': 5.083}
    for name, (base, spread) in spreads.items():
        noise = np.random.default_rng([zlib.crc32(name.encode()), seed]).standard_normal(out[name].shape)
        drawn = base * np.exp(spread * noise) if base else spread * noise
        out[name] = __import__('jax').numpy.asarray(drawn.astype(out[name].dtype))
    for name, factor in factors.items():
        out[name] = (out[name] * factor).astype(out[name].dtype)
    return out
```

```python
from contextlib import ExitStack

import concourse.bass as bass
from concourse import mybir

P = 128
F32 = mybir.dt.float32
F32R = mybir.dt.float32r
ALU = mybir.AluOpType
ACT = mybir.ActivationFunctionType
AX = mybir.AxisListType

V, X, BC, U, Z, OUT, PLE, FF, GATE = 0, 2, 4, 5, 7, 9, 13, 14, 30
EPS = 1e-6


def build_layer(nc, a, out):
    _, _, SEQ, D = (1,) + tuple(a["x"].shape)
    NS = SEQ // P
    KT = D // P
    W = a["gm_v_norm_g"].shape[1]
    GH = a["gm_ws"].shape[1]
    R = a["ssd_a_log"].shape[1]
    G2 = 2
    RG = R // G2
    HD = W // R
    DF = a["w_ff1"].shape[2]
    NE = DF // 512
    assert (NS, KT, W, GH, RG, HD, NE) == (4, 8, 1024, 8, 8, 64, 8)
    LAST = FF + 2 * NE
    assert LAST == GATE

    w_in = a["w_in"][0].rearrange("(k p) n -> p k n", p=P)
    w_out = a["w_out"][0].rearrange("(k p) n -> p k n", p=P)
    w_ff1 = a["w_ff1"][0].rearrange("(k p) n -> p k n", p=P)
    w_ff2 = a["w_ff2"][0].rearrange("(k p) n -> p k n", p=P)
    w_gate = a["w_ple_gate"][0].rearrange("(k p) n -> p k n", p=P)
    w_ple = a["w_ple_proj"][0].rearrange("(k p) n -> p k n", p=P)
    x_dram = a["x"][0].rearrange("(s p) n -> p s n", p=P)
    out_dram = out[0].rearrange("(s p) n -> p s n", p=P)
    p_dram = a["p"][0, 0].rearrange("(s p) n -> p s n", p=P)

    with ExitStack() as ctx:
        def sb(name, shape, dt=F32, where=ctx):
            return where.enter_context(nc.sbuf_tensor(name, shape, dt))

        def sem(name):
            return ctx.enter_context(nc.semaphore(name))

        w_raw = sb("w_raw", [P, 4, 2, 512])
        w_hi = sb("w_hi", [P, 2, 8, 512], F32R)
        w_lo = sb("w_lo", [P, 2, 8, 512], F32R)
        a_hi = sb("a_hi", [P, KT, SEQ], F32R)
        a_lo = sb("a_lo", [P, KT, SEQ], F32R)
        h = sb("h", [P, NS, D])
        y = sb("y", [P, NS, D])
        gain = sb("gain", [P, 2, D])
        tmp = sb("tmp", [P, 4, 512])
        ident = sb("ident", [P, P])
        upper = sb("upper", [P, P])
        after = sb("after", [P, P])
        after_r = sb("after_r", [P, P], F32R)
        ones = sb("ones", [P, P])
        eps = sb("eps", [P, 1])
        rows = sb("rows", [P, P])
        cols = sb("cols", [P, 68])
        a_log = sb("a_log", [P, R])
        d_skip = sb("d_skip", [P, R])
        dt_b = sb("dt_b", [R, 1])
        w_dt = sb("w_dt", [P, KT, R])
        dt = sb("dt", [P, NS, R])
        e_a = sb("e_a", [P, R])
        dA = sb("dA", [P, NS, R])
        dA_hi = sb("dA_hi", [P, NS, R], F32R)
        dA_lo = sb("dA_lo", [P, NS, R])
        decay = sb("decay", [P, 3, NS, R])
        ssq = sb("ssq", [P, 16])
        rms = sb("rms", [P, 16])
        rstd = sb("rstd", [P, 16])
        v_ssq = sb("v_ssq", [P, NS, GH])
        v_rms = sb("v_rms", [P, NS, GH])
        v_rstd = sb("v_rstd", [P, NS, GH])
        m_ssq = sb("m_ssq", [P, 12])
        m_rms = sb("m_rms", [P, 12])
        m_rstd = sb("m_rstd", [P, 12])
        with ExitStack() as early:
            conv = sb("conv", [P, 2, 512], where=early)
            xs_t = sb("xs_t", [P, 2, 512], where=early)
        p_hi = sb("p_hi", [P, 2, SEQ], F32R)
        p_lo = sb("p_lo", [P, 2, SEQ], F32R)
        with ExitStack() as early:
            with ExitStack() as first:
                dtT = sb("dtT", [R, SEQ], where=first)
                dts = sb("dts", [P, 5, NS * R], where=first)
            lm = sb("lm", [P, RG, P], where=early)
            cbm = sb("cbm", [P, P], where=early)
            bcT = sb("bcT", [P, 4, SEQ], where=early)
            with ExitStack() as first:
                wsT = sb("wsT", [P, GH, P], where=first)
            b_nat = sb("b_nat", [P, G2, NS, P], where=early)
            xdt = sb("xdt", [P, 512], where=early)
            xdd = sb("xdd", [P, 512], where=early)
            seg_hi = sb("seg_hi", [P, 8, P], F32R, where=early)
            seg_lo = sb("seg_lo", [P, 8, P], F32R, where=early)
            carry = sb("carry", [P, 512], where=early)
        b_hi = sb("b_hi", [P, KT, SEQ], F32R)
        b_lo = sb("b_lo", [P, KT, SEQ], F32R)

        acc = ctx.enter_context(nc.psum_tensor("acc", [P, 4, 512], F32))
        side = ctx.enter_context(nc.psum_tensor("side", [P, 4, 512], F32))

        w_landed = [sem(f"w_landed{i}") for i in range(4)]
        hi_ready = sem("hi_ready")
        lo_ready = sem("lo_ready")
        acc_full = sem("acc_full")
        act_evac = sem("act_evac")
        dve_evac = sem("dve_evac")
        side_full = [sem(f"side_full{i}") for i in range(4)]
        side_free = [sem(f"side_free{i}") for i in range(4)]
        x_landed = [sem(f"x_landed{i}") for i in range(NS)]
        gain_landed = [sem(f"gain_landed{i}") for i in range(2)]
        rows_landed, small_landed = sem("rows_landed"), sem("small_landed")
        ws_landed = sem("ws_landed")
        p_landed = sem("p_landed")
        ssq_ready, rms_ready = sem("ssq_ready"), sem("rms_ready")
        rstd_ready, xn_ready = sem("rstd_ready"), sem("xn_ready")
        xt_hi, xt_lo = sem("xt_hi"), sem("xt_lo")
        consts_ready = sem("consts_ready")
        eps_ready = sem("eps_ready")
        after_ready = sem("after_ready")
        v_sq, v_sum = sem("v_sq"), sem("v_sum")
        v_rms_ready, v_rstd_ready = sem("v_rms_ready"), sem("v_rstd_ready")
        v_scaled, v_ready = sem("v_scaled"), sem("v_ready")
        conv_begun, silu_done = sem("conv_begun"), sem("silu_done")
        conv_step = sem("conv_step")
        wdt_zero, wdt_ready = sem("wdt_zero"), sem("wdt_ready")
        dtT_ready, dt_step, dt_exp = sem("dtT_ready"), sem("dt_step"), sem("dt_exp")
        ea_ready, dt_ready, dA_ready = sem("ea_ready"), sem("dt_ready"), sem("dA_ready")
        seg_ready, xdt_ready, xsd_ready = sem("seg_ready"), sem("xdt_ready"), sem("xsd_ready")
        exp_done, cbm_ready, lm_ready = sem("exp_done"), sem("cbm_ready"), sem("lm_ready")
        ssd_step = sem("ssd_step")
        ya_mul, yb_mul = sem("ya_mul"), sem("yb_mul")
        m_ssq_ready, m_rms_ready = sem("m_ssq_ready"), sem("m_rms_ready")
        m_rstd_ready = sem("m_rstd_ready")
        ya_norm, yb_norm = sem("ya_norm"), sem("yb_norm")
        yt_hi, yt_lo = sem("yt_hi"), sem("yt_lo")
        pt_hi, pt_lo = sem("pt_hi"), sem("pt_lo")
        sq_ready, hid_hi, hid_lo = sem("sq_ready"), sem("hid_hi"), sem("hid_lo")
        gated, h_final, o_ready = sem("gated"), sem("h_final"), sem("o_ready")
        out_done = sem("out_done")

        kind = {}
        for b in range(GATE + 2):
            if b in (OUT, OUT + 1, OUT + 2, OUT + 3):
                kind[b] = "pair_dve"
            elif b == PLE:
                kind[b] = "pair_act"
            elif FF <= b < GATE:
                kind[b] = "pair_dve" if b == GATE - 1 or (b > FF and (b - FF) % 2 == 0) else "one_act"
            elif X <= b < U:
                kind[b] = "one_dve"
            else:
                kind[b] = "one_act"
        before = {b: 4 * sum(kind[c][-3:] == kind[b][-3:] for c in range(b)) for b in kind}

        def emptied(b, s, shift=0):
            return (act_evac if kind[b].endswith("act") else dve_evac), before[b] + s + 1 + shift

        def last_user(b, s):
            pair, prev = kind[b].startswith("pair"), kind[b - 1].startswith("pair") if b else False
            if pair:
                if s >= 2:
                    return b, s - 2
                return b - 1, (s + 2 if prev else 2 * s + 1)
            return b - 1, (2 + s // 2 if prev else s)

        plan = [("cols", 3)]
        plan += [(("xt", 0, s, q), (2 * s + q) % 4) for s in range(NS) for q in range(2)]
        plan += [(("ws", i), i) for i in range(2)]
        for t in range(9, 19):
            if t < 17:
                plan.append((("xs", t - 9), (t - 9) % 2))
            if t == 10:
                plan.append(("dt", 2))
            if t == 11:
                plan.append(("dt_nat", 3))
            if t == 13:
                plan.append(("decay", 3))
            if 14 <= t < 18:
                plan += [(("mix", 2 * (t - 14) + i), 2 + i) for i in range(2)]
            if t >= 17:
                plan.append((("b_nat", t - 17), t - 17))
        for j in range(8):
            plan += [(("cb", j), 3), (("seg", j, 0), 0), (("seg", j, 1), 1)]
            if j % 4 > 0:
                plan.append((("off", j), 3))
            plan.append((("diag", j), 2))
            if j % 4 < 3:
                plan.append((("state", j), 0))
        plan += [(("yt", half, s), s) for half in range(2) for s in range(NS)]
        plan += [(("yt", 2 + q, s), (2 * s + q) % 4) for s in range(NS) for q in range(2)]
        plan += [(("pt", k), k) for k in range(2)]
        plan += [(("xt", n, s, q), (2 * s + q) % 4) for n in (1, 2) for s in range(NS) for q in range(2)]
        fills, order = {}, [0] * 4
        for name, bank in plan:
            fills[name] = (bank, order[bank])
            order[bank] += 1

        def wait_full(eng, name):
            bank, n = fills[name]
            eng.wait_ge(side_full[bank], n + 1)
            return side[:, bank, :]

        def wait_filled(eng, name):
            bank, n = fills[name]
            eng.wait_ge(side_full[bank], n + 1)

        def wait_free(eng, name):
            bank, n = fills[name]
            eng.wait_ge(side_free[bank], n + 1)

        def freed(ins, name):
            ins.then_inc(side_free[fills[name][0]], 1)

        block = ctx.enter_context(nc.Block())

        @block.sync
        def _(sp):
            def piece(b, p, src, dst, shift=0):
                if not (isinstance(b, int) and b == 0):
                    sp.wait_ge(lo_ready, 4 * (b - 1) + p + 1 + shift)
                sp.dma_start(dst, src).then_inc(w_landed[p], 16)

            def load_k(b, w, c0, shift=0):
                for p in range(4):
                    piece(b, p, w[:, 2 * p:2 * p + 2, bass.ds(c0, 512)], w_raw[:, p], shift)

            def load_rows(b, w, k0, shift=0):
                for p in range(4):
                    piece(b, p, w[:, bass.ds(k0 + p, 1), :],
                          w_raw[:, p].rearrange("p a n -> p (a n)")[:, None, :], shift)

            def load_gain(g, slot):
                sp.dma_start(gain[:, slot, :], g.partition_broadcast(P)).then_inc(gain_landed[slot], 16)

            sp.dma_start(h[:, 0, :], x_dram[:, 0, :]).then_inc(x_landed[0], 16)
            load_gain(a["norm_mix_g"][0], 0)
            cw = a["ssd_conv_w"][0].rearrange("k (i p) -> (k i) p", p=P)
            sp.dma_start(rows[0:48, :], cw).then_inc(rows_landed, 16)
            sp.dma_start(rows[48:60, :], a["ssd_conv_b"][0].rearrange("(i p) -> i p", p=P)).then_inc(rows_landed, 16)
            sp.dma_start(rows[60:68, :], a["gm_bs"][0]).then_inc(rows_landed, 16)
            for s in range(1, NS):
                sp.dma_start(h[:, s, :], x_dram[:, s, :]).then_inc(x_landed[s], 16)
            load_k(0, w_in, W)
            sp.dma_start(a_log[:], a["ssd_a_log"][0].partition_broadcast(P)).then_inc(small_landed, 16)
            sp.dma_start(d_skip[:], a["ssd_d"][0].partition_broadcast(P)).then_inc(small_landed, 16)
            sp.dma_start(dt_b[:], a["ssd_dt_bias"][0].rearrange("(p o) -> p o", o=1)).then_inc(small_landed, 16)
            sp.dma_start(w_dt[:], w_in[:, :, 4 * W + 512:4 * W + 512 + R]).then_inc(small_landed, 16)
            sp.dma_start(y[:, 0:1, :].rearrange("p a (g s) -> p (a g) s", g=GH),
                         a["gm_ws"][0].rearrange("g t s -> t g s")).then_inc(ws_landed, 16)
            load_gain(a["gm_v_norm_g"][0], 1)
            load_k(V + 1, w_in, W + 512)
            for i in range(3):
                load_k(X + i, w_in, 3 * W + 512 * i)
            sp.wait_ge(xn_ready, NS)
            load_gain(a["gm_out_norm_g"][0], 0)
            load_k(U, w_in, 0)
            sp.wait_ge(v_ready, NS)
            load_gain(a["ssd_norm_g"][0], 1)
            load_k(U + 1, w_in, 512)
            for i in range(2):
                load_k(Z + i, w_in, 2 * W + 512 * i)
            load_rows(OUT, w_out, 0)
            sp.wait_ge(ya_norm, NS)
            load_gain(a["norm_mlp_g"][0], 0)
            load_rows(OUT + 1, w_out, 4)
            for s in range(NS):
                wait_filled(sp, ("yt", 1, s))
                sp.dma_start(h[:, s, :], x_dram[:, s, :]).then_inc(x_landed[s], 16)
            load_rows(OUT + 2, w_out, 8)
            sp.wait_ge(yb_mul, 8)
            sp.dma_start(tmp[:, 0:2, :].rearrange("p a (b n) -> p (a b) n", b=2), p_dram).then_inc(p_landed, 16)
            load_rows(OUT + 3, w_out, 12)
            sp.wait_ge(yb_norm, 8)
            load_gain(a["ple_norm_g"][0], 1)
            for p in range(4):
                piece(PLE, p, w_ple[:, p // 2, 512 * (p % 2):512 * (p % 2) + 512], w_raw[:, p, 0, :])
            load_k(FF, w_ff1, 0)
            with sp.Fori(0, 3) as i:
                b = FF + 1
                for q in range(2):
                    load_k(b + 2 * q, w_ff1, i * 1024 + 512 * (q + 1), 16 * i)
                    load_rows(b + 2 * q + 1, w_ff2, i * 8 + 4 * q, 16 * i)
            load_k(LAST - 3, w_ff1, 7 * 512)
            load_rows(LAST - 2, w_ff2, 6 * 4)
            load_rows(LAST - 1, w_ff2, 7 * 4)
            sp.wait_ge(xn_ready, 2 * NS)
            load_gain(a["final_norm_g"], 0)
            for i in range(2):
                load_k(GATE + i, w_gate, 512 * i)
            for s in range(NS):
                sp.wait_ge(o_ready, s + 1)
                sp.dma_start(out_dram[:, s, :], h[:, s, :]).then_inc(out_done, 16)
            sp.wait_ge(out_done, 16 * NS)

        @block.gpsimd
        def _(pool):
            pool.memset(ident[:], 0.0).then_inc(consts_ready, 1)
            pool.memset(ones[:], 1.0).then_inc(consts_ready, 1)
            pool.wait_ge(consts_ready, 2)
            pool.affine_select(out=ident[:], in_=ident[:], compare_op=ALU.not_equal, fill=1.0, base=0,
                               pattern=[[-1, P]], channel_multiplier=1).then_inc(consts_ready, 1)
            pool.affine_select(out=upper[:], in_=ones[:], compare_op=ALU.is_ge, fill=0.0, base=0,
                               pattern=[[1, P]], channel_multiplier=-1).then_inc(consts_ready, 1)
            pool.affine_select(out=after[:], in_=ones[:], compare_op=ALU.is_ge, fill=0.0, base=-1,
                               pattern=[[-1, P]], channel_multiplier=1).then_inc(consts_ready, 1)
            for s in range(NS):
                pool.wait_ge(act_evac, 4 + s + 1)
                if s < 2:
                    pool.wait_ge(xn_ready, 3 + s)
                else:
                    pool.wait_ge(v_sum, s - 1)
                pool.tensor_tensor(tmp[:, 2 * (s % 2):2 * (s % 2) + 2, :].rearrange("p a n -> p (a n)"),
                                   h[:, s, :], h[:, s, :], ALU.mult).then_inc(v_sq, 1)
            for s in range(NS):
                if s == 0:
                    pool.wait_ge(gain_landed[1], 16)
                pool.wait_ge(v_scaled, s + 1)
                pool.tensor_tensor(h[:, s, :], h[:, s, :], gain[:, 1, :], ALU.mult).then_inc(v_ready, 1)
            pool.wait_ge(dA_ready, 2)
            for j in range(8):
                g, c = divmod(j, 4)
                up = upper[:, None, :].broadcast_to([P, 8, P])
                heads = slice(g * RG, g * RG + RG)
                if j:
                    wait_filled(pool, ("seg", j - 1, 1))
                else:
                    wait_filled(pool, "dt")
                pool.tensor_tensor(seg_hi[:], up, dA_hi[:, c, heads].bitcast(F32)[:, :, None].broadcast_to([P, 8, P]),
                                   ALU.mult).then_inc(seg_ready, 1)
                pool.tensor_tensor(seg_lo[:], up, dA_lo[:, c, heads][:, :, None].broadcast_to([P, 8, P]),
                                   ALU.mult).then_inc(seg_ready, 1)
                if j == 0:
                    for i in range(8):
                        wait_free(pool, ("xs", i))
                    wait_free(pool, "decay")
                else:
                    wait_filled(pool, ("diag", j - 1))
                    if (j - 1) % 4 < 3:
                        wait_filled(pool, ("state", j - 1))
                xs = y[:, c, 512 * g:512 * g + 512].rearrange("p (r d) -> p r d", r=RG)
                xdt_v, xdd_v = (t[:].rearrange("p (r d) -> p r d", r=RG) for t in (xdt, xdd))
                pool.tensor_tensor(xdt_v, xs, dt[:, c, heads][:, :, None].broadcast_to([P, RG, HD]),
                                   ALU.mult).then_inc(xdt_ready, 1)
                pool.wait_ge(xdt_ready, 2 * j + 1)
                pool.tensor_tensor(xdd_v, xdt_v, decay[:, 1, c, heads][:, :, None].broadcast_to([P, RG, HD]),
                                   ALU.mult).then_inc(xdt_ready, 1)
                if j == 0:
                    pool.wait_ge(small_landed, 16 * 4)
                pool.tensor_tensor(xs, xs, d_skip[:, heads][:, :, None].broadcast_to([P, RG, HD]),
                                   ALU.mult).then_inc(xsd_ready, 1)

        @block.scalar
        def _(act):
            def split_hi(b, p, shift=0, trip=0):
                half = b % 2
                act.wait_ge(w_landed[p], 16 * (b + 1) + 64 * trip)
                if b >= 2:
                    act.wait_ge(acc_full, 4 * (b - 1) + shift)
                n = 1 if b == PLE else 2
                act.activation(w_hi[:, half, 2 * p:2 * p + n, :], w_raw[:, p, 0:n, :], ACT.Copy).then_inc(hi_ready, 1)

            def sums(n, s):
                i = 4 * n + s
                junk = xs_t[:] if n == 3 else tmp[:, 2 * (s % 2):2 * (s % 2) + 2, :]
                if n == 0:
                    act.wait_ge(x_landed[s], 16)
                    if s == 0:
                        act.wait_ge(eps_ready, 1)
                    if s >= 2:
                        act.wait_ge(ssq_ready, s - 1)
                elif n == 3:
                    act.wait_ge(h_final, 4 + s + 1)
                    if s:
                        act.wait_ge(ssq_ready, i)
                else:
                    b = OUT + 3 if n == 1 else LAST - 1
                    act.wait_ge(*emptied(b, s))
                    if s >= 2:
                        wait_filled(act, ("xt", n, s - 2, 1))
                    elif n == 1:
                        for q in range(2):
                            wait_filled(act, ("pt", q))
                    else:
                        act.wait_ge(hid_lo, 4 * NE)
                act.activation(junk.rearrange("p a n -> p (a n)"), h[:, s, :], ACT.Square,
                               accum_out=ssq[:, i:i + 1]).then_inc(ssq_ready, 1)
                act.wait_ge(ssq_ready, i + 1)
                act.activation(rms[:, i:i + 1], ssq[:, i:i + 1], ACT.Sqrt, bias=eps[:], scale=1.0 / D
                               ).then_inc(rms_ready, 1)

            def xt_evac(n, s):
                hi = a_hi if n == 0 else b_hi
                for q in range(2):
                    bank = wait_full(act, ("xt", n, s, q))
                    if n == 2 and s == 0 and q == 0:
                        act.wait_ge(acc_full, 4 * (LAST - 2))
                    act.activation(hi[:, 4 * q:4 * q + 4, s * P:s * P + P],
                                   bank.rearrange("p (k n) -> p k n", k=4), ACT.Copy).then_inc(xt_hi, 1)

            def yt_evac(part, s):
                bank = wait_full(act, ("yt", part, s))
                hi = a_hi if part < 2 else b_hi
                if part == 0 and s == 0:
                    act.wait_ge(acc_full, 4 * OUT)
                if part == 2 and s == 0:
                    wait_free(act, ("diag", 7))
                q = part % 2
                act.activation(hi[:, 4 * q:4 * q + 4, s * P:s * P + P],
                               bank.rearrange("p (k n) -> p k n", k=4), ACT.Copy).then_inc(yt_hi, 1)

            def relu_evac(b, s, e, trip=0):
                n = 4 * e + s
                act.wait_ge(acc_full, 4 * b + s + 1 + 16 * trip)
                if isinstance(e, int) and n < 2:
                    wait_filled(act, ("xt", 1, 2 + s, 1))
                else:
                    act.wait_ge(sq_ready, n - 1 + 8 * trip)
                act.activation(tmp[:, s % 2, :], acc[:, s, :], ACT.Relu).then_inc(act_evac, 1)

            def hid_evac(s, e, trip=0):
                n = 4 * e + s
                act.wait_ge(sq_ready, n + 1 + 8 * trip)
                act.activation(a_hi[:, 4 * (e % 2) + s, :], tmp[:, 2 + s % 2, :], ACT.Copy).then_inc(hid_hi, 1)

            for s in range(NS):
                sums(0, s)
                split_hi(0, s)
                if s:
                    xt_evac(0, s - 1)
            xt_evac(0, NS - 1)

            for t in range(4 * OUT):
                b, s = divmod(t, 4)
                split_hi(b + 1, s)
                if t == 8:
                    act.wait_ge(v_sum, NS)
                    act.activation(v_rms[:], v_ssq[:], ACT.Sqrt, bias=eps[:], scale=1.0 / P).then_inc(v_rms_ready, 1)
                if 10 <= t < 18:
                    bank = wait_full(act, ("xs", t - 10))
                    if t == 10:
                        wait_free(act, ("ws", 1))
                    ins = act.activation(y[:, :, (t - 10) * P:(t - 10) * P + P],
                                         bank.rearrange("p (c n) -> p c n", c=NS), ACT.Copy)
                    freed(ins, ("xs", t - 10))
                if t == 11:
                    bank = wait_full(act, "dt")
                    act.wait_ge(small_landed, 16 * 4)
                    ins = act.activation(dtT[:], bank[0:R, :], ACT.Identity, bias=dt_b[:])
                    freed(ins, "dt")
                if t == 12:
                    act.activation(e_a[:], a_log[:], ACT.Exp).then_inc(ea_ready, 1)
                    act.wait_ge(dt_step, 2)
                    act.activation(dts[:, 2, :], dts[:, 1, :], ACT.Exp).then_inc(dt_exp, 1)
                if t == 14:
                    bank = wait_full(act, "decay")
                    ins = act.activation(decay[:].rearrange("p a c r -> p (a c r)"), bank[:, 0:3 * NS * R], ACT.Exp)
                    freed(ins, "decay")
                if 15 <= t < 19:
                    for i in range(2):
                        head = 2 * (t - 15) + i
                        bank = wait_full(act, ("mix", head))
                        ins = act.activation(h[:, :, head * P:head * P + P], bank.rearrange("p (c n) -> p c n", c=NS),
                                             ACT.Identity, bias=cols[:, 60 + head:61 + head])
                        freed(ins, ("mix", head))
                if 18 <= t < 20:
                    bank = wait_full(act, ("b_nat", t - 18))
                    ins = act.activation(b_nat[:, t - 18].rearrange("p c n -> p (c n)"), bank, ACT.Copy)
                    freed(ins, ("b_nat", t - 18))
                if t >= 20 and t % 2 == 0:
                    j = (t - 20) // 2
                    if j:
                        wait_filled(act, ("diag", j - 1))
                    for i in range(2):
                        bank = wait_full(act, ("seg", j, i))
                        ins = act.activation(lm[:, 4 * i:4 * i + 4, :].rearrange("p r n -> p (r n)"), bank, ACT.Exp)
                        freed(ins, ("seg", j, i))
                if t in (28, 29, 30, 31):
                    i = t - 28
                    act.wait_ge(ya_mul, 4 + i + 1)
                    if i:
                        act.wait_ge(m_ssq_ready, i)
                    act.activation(conv[:].rearrange("p a n -> p (a n)"), h[:, i, :], ACT.Square,
                                   accum_out=m_ssq[:, i:i + 1]).then_inc(m_ssq_ready, 1)
                if t == 31:
                    act.wait_ge(m_ssq_ready, 4)
                    act.activation(m_rms[:, 0:4], m_ssq[:, 0:4], ACT.Sqrt, bias=eps[:], scale=1.0 / W
                                   ).then_inc(m_rms_ready, 1)
                if 32 <= t < 36:
                    i = t - 32
                    act.wait_ge(yb_mul, i + 1)
                    act.wait_ge(m_ssq_ready, 4 + i)
                    act.activation(conv[:, 0, :], y[:, i, 0:512], ACT.Square,
                                   accum_out=m_ssq[:, 4 + i:5 + i]).then_inc(m_ssq_ready, 1)
                if t == 35:
                    act.wait_ge(m_ssq_ready, 8)
                    act.activation(m_rms[:, 4:8], m_ssq[:, 4:8], ACT.Sqrt, bias=eps[:], scale=2.0 / W
                                   ).then_inc(m_rms_ready, 1)
                act.wait_ge(acc_full, t + 1)
                if b < X:
                    if t < 4:
                        wait_filled(act, ("xt", 0, s, 1))
                    act.activation(h[:, s, 512 * b:512 * b + 512], acc[:, s, :], ACT.Gelu).then_inc(act_evac, 1)
                elif b < U:
                    i = t - 4 * X
                    if i == 0:
                        wait_free(act, "cols")
                    if i >= 2:
                        act.wait_ge(silu_done, i - 1)
                    act.activation(conv[:, i % 2, :], acc[:, s, :], ACT.Copy, scale=cols[:, 36 + i:37 + i]
                                   ).then_inc(conv_begun, 1)
                    act.wait_ge(*emptied(b, s))
                    if i < 8:
                        if i >= 2:
                            wait_filled(act, ("xs", i - 2))
                        dst = xs_t[:, i % 2, :]
                    else:
                        dst = bcT[:, i - 8, :]
                    act.activation(dst, conv[:, i % 2, :], ACT.Silu, bias=cols[:, 48 + i:49 + i]).then_inc(silu_done, 1)
                elif b < Z:
                    i = t - 4 * U
                    if i < 4:
                        act.wait_ge(v_sum, NS)
                    else:
                        act.wait_ge(ya_mul, i - 3)
                    act.activation(tmp[:, s, :], acc[:, s, :], ACT.Gelu).then_inc(act_evac, 1)
                else:
                    i = t - 4 * Z
                    act.wait_ge(ya_mul, 5 + i) if i < 4 else act.wait_ge(yb_mul, i - 3)
                    act.activation(tmp[:, s, :], acc[:, s, :], ACT.Silu).then_inc(act_evac, 1)

            for i in range(4):
                act.wait_ge(yb_mul, 4 + i + 1)
                act.wait_ge(m_ssq_ready, 8 + i)
                act.activation(conv[:, 0, :], y[:, i, 512:1024], ACT.Square,
                               accum_out=m_ssq[:, 8 + i:9 + i]).then_inc(m_ssq_ready, 1)
            act.wait_ge(m_ssq_ready, 12)
            act.activation(m_rms[:, 8:12], m_ssq[:, 8:12], ACT.Sqrt, bias=eps[:], scale=2.0 / W
                           ).then_inc(m_rms_ready, 1)
            for s in range(NS):
                yt_evac(0, s)
            for b in range(OUT, OUT + 4):
                for s in range(4):
                    split_hi(b + 1, s)
                    t = 4 * b + s
                    if b == OUT and s == 1:
                        for i in range(NS):
                            yt_evac(1, i)
                    if 41 <= t < 45:
                        for q in range(2):
                            yt_evac(2 + q, t - 41)
                    if t == 45:
                        for k in range(2):
                            bank = wait_full(act, ("pt", k))
                            act.activation(p_hi[:, k, :], bank, ACT.Copy).then_inc(pt_hi, 1)
                    if b == OUT + 3:
                        if s >= 2:
                            xt_evac(1, s - 2)
                        sums(1, s)

            for s in range(4):
                split_hi(FF, s)
                if s == 0:
                    xt_evac(1, 2)
                if s == 2:
                    xt_evac(1, 3)
                act.wait_ge(acc_full, 4 * PLE + s + 1)
                if s == 0:
                    for i in range(NS):
                        wait_filled(act, ("yt", 3, i))
                i = 2 * (s % 2)
                act.activation(y[:, s, :].rearrange("p (a n) -> p a n", a=2), acc[:, i:i + 2, :],
                               ACT.Copy).then_inc(act_evac, 1)

            def ff1(b, e, trip=0):
                for s in range(4):
                    split_hi(b + 1, s, 16 * trip, trip=trip)
                    relu_evac(b, s, e, trip)
                    hid_evac(s, e, trip)

            def ff2(b, trip=0):
                for s in range(4):
                    split_hi(b + 1, s, 16 * trip, trip=trip)

            ff1(FF, 0)
            with act.Fori(0, 3) as i:
                for q in range(2):
                    ff1(FF + 1 + 2 * q, 1 + q, i)
                    ff2(FF + 2 + 2 * q, i)
            ff1(LAST - 3, 7)
            ff2(LAST - 2)
            for s in range(4):
                split_hi(GATE, s)
                if s >= 2:
                    xt_evac(2, s - 2)
                sums(2, s)

            for i in range(8):
                b, s = GATE + i // 4, i % 4
                if b == GATE:
                    split_hi(GATE + 1, s)
                if i == 0:
                    xt_evac(2, 2)
                if i == 2:
                    xt_evac(2, 3)
                act.wait_ge(acc_full, 4 * b + s + 1)
                if i >= 2:
                    act.wait_ge(gated, i - 1)
                act.activation(conv[:, i % 2, :], acc[:, s, :], ACT.Sigmoid).then_inc(act_evac, 1)
                if b > GATE:
                    sums(3, s)

        @block.vector
        def _(dve):
            def split_lo(b, p, trip=0):
                half = b % 2
                dve.wait_ge(hi_ready, 4 * b + p + 1 + 16 * trip)
                n = 1 if b == PLE else 2
                dve.tensor_tensor(w_lo[:, half, 2 * p:2 * p + n, :], w_raw[:, p, 0:n, :],
                                  w_hi[:, half, 2 * p:2 * p + n, :].bitcast(F32), ALU.subtract).then_inc(lo_ready, 1)

            def normed(n, s):
                i = 4 * n + s
                dve.wait_ge(rms_ready, i + 1)
                dve.reciprocal(rstd[:, i:i + 1], rms[:, i:i + 1]).then_inc(rstd_ready, 1)
                dve.wait_ge(rstd_ready, i + 1)
                slot, use = ((0, 1), (0, 3), (1, 3), (0, 4))[n]
                if s == 0:
                    dve.wait_ge(gain_landed[slot], 16 * use)
                if n in (0, 3):
                    dst = h[:, s, :]
                else:
                    dst = tmp[:, 2 * (s % 2):2 * (s % 2) + 2, :].rearrange("p a n -> p (a n)")
                dve.scalar_tensor_tensor(dst, h[:, s, :], rstd[:, i:i + 1], gain[:, slot, :], ALU.mult, ALU.mult
                                         ).then_inc(o_ready if n == 3 else xn_ready, 1)

            def xt_evac(n, s):
                hi, lo = (a_hi, a_lo) if n == 0 else (b_hi, b_lo)
                for q in range(2):
                    name = ("xt", n, s, q)
                    bank = side[:, fills[name][0], :]
                    dve.wait_ge(xt_hi, 8 * n + 2 * s + q + 1)
                    at = (slice(None), slice(4 * q, 4 * q + 4), slice(s * P, s * P + P))
                    dve.tensor_tensor(lo[at], bank.rearrange("p (k n) -> p k n", k=4), hi[at].bitcast(F32),
                                      ALU.subtract).then_inc(side_free[fills[name][0]], 1)

            def yt_evac(part, s, n):
                name = ("yt", part, s)
                bank = side[:, fills[name][0], :]
                hi, lo = (a_hi, a_lo) if part < 2 else (b_hi, b_lo)
                q = part % 2
                dve.wait_ge(yt_hi, n + 1)
                at = (slice(None), slice(4 * q, 4 * q + 4), slice(s * P, s * P + P))
                dve.tensor_tensor(lo[at], bank.rearrange("p (k n) -> p k n", k=4), hi[at].bitcast(F32),
                                  ALU.subtract).then_inc(side_free[fills[name][0]], 1)

            def add_group(b, s, base=None, trip=0):
                dve.wait_ge(acc_full, 4 * b + s + 1 + 16 * trip)
                if b == OUT:
                    dve.wait_ge(x_landed[s], 32)
                else:
                    prev = before[b] + s + 1 - 4
                    dve.wait_ge(dve_evac, prev + 8 * trip)
                i = 2 * (s % 2)
                hs = h[:, s, :].rearrange("p (a n) -> p a n", a=2)
                dve.tensor_tensor(hs, hs, acc[:, i:i + 2, :], ALU.add).then_inc(dve_evac, 1)

            dve.memset(eps[:], EPS).then_inc(eps_ready, 1)
            dve.memset(seg_hi[:].bitcast(F32), 0.0).then_inc(wdt_zero, 1)
            dve.memset(seg_lo[:].bitcast(F32), 0.0).then_inc(wdt_zero, 1)
            for s in range(NS):
                normed(0, s)
                if s == 0:
                    bank = wait_full(dve, "cols")
                    freed(dve.tensor_copy(cols[:], bank[:, 0:68]), "cols")
                if s:
                    xt_evac(0, s - 1)
                split_lo(0, s)
            xt_evac(0, NS - 1)
            dve.wait_ge(consts_ready, 5)
            dve.tensor_copy(after_r[:], after[:]).then_inc(after_ready, 1)
            dve.wait_ge(small_landed, 16 * 4)
            dve.wait_ge(wdt_zero, 2)
            dve.tensor_copy(seg_hi[:, :, 0:R], w_dt[:]).then_inc(wdt_ready, 1)
            dve.wait_ge(wdt_ready, 1)
            dve.tensor_tensor(seg_lo[:, :, 0:R], w_dt[:], seg_hi[:, :, 0:R].bitcast(F32), ALU.subtract
                              ).then_inc(wdt_ready, 1)

            step = [0]

            def chain(ins):
                step[0] += 1
                ins.then_inc(dt_step, 1)
                dve.wait_ge(dt_step, step[0])

            done = [0]

            def ssd(ins):
                done[0] += 1
                ins.then_inc(ssd_step, 1)
                dve.wait_ge(ssd_step, done[0])

            for t in range(4 * OUT):
                b, s = divmod(t, 4)
                split_lo(b + 1, s)
                if t == 1:
                    for i in range(2):
                        bank = wait_full(dve, ("ws", i))
                        up = upper[:, None, :].broadcast_to([P, 4, P])
                        freed(dve.tensor_tensor(wsT[:, 4 * i:4 * i + 4, :], bank.rearrange("p (g n) -> p g n", g=4),
                                                up, ALU.mult), ("ws", i))
                if 5 <= t < 9:
                    i = t - 5
                    dve.wait_ge(v_sq, i + 1)
                    dve.tensor_reduce(v_ssq[:, i, :], tmp[:, 2 * (i % 2):2 * (i % 2) + 2, :].rearrange(
                        "p a (g n) -> p (a g) n", n=P), AX.X, ALU.add).then_inc(v_sum, 1)
                if t == 9:
                    dve.wait_ge(v_rms_ready, 1)
                    dve.reciprocal(v_rstd[:], v_rms[:]).then_inc(v_rstd_ready, 1)
                    dve.wait_ge(v_rstd_ready, 1)
                    for i in range(NS):
                        hv = h[:, i, :].rearrange("p (g n) -> p g n", g=GH)
                        dve.tensor_tensor(hv, hv, v_rstd[:, i, :][:, :, None].broadcast_to([P, GH, P]),
                                          ALU.mult).then_inc(v_scaled, 1)
                if t == 12:
                    bank = wait_full(dve, "dt_nat")
                    d = [dts[:, i, :] for i in range(5)]
                    ins = dve.tensor_copy(d[0], bank[:, 0:NS * R])
                    freed(ins, "dt_nat")
                    wait_free(dve, "dt_nat")
                    chain(dve.tensor_scalar(d[4], d[0], 0.0, None, ALU.max))
                    chain(dve.scalar_tensor_tensor(d[1], d[0], -1.0, d[0], ALU.mult, ALU.min))
                    dve.wait_ge(dt_exp, 1)
                    chain(dve.tensor_scalar(d[0], d[2], 2.0, None, ALU.add))
                    chain(dve.reciprocal(d[1], d[0]))
                    chain(dve.tensor_tensor(d[2], d[2], d[1], ALU.mult))
                    chain(dve.tensor_tensor(d[0], d[2], d[2], ALU.mult))
                    chain(dve.tensor_scalar(d[1], d[0], 1.0 / 17, None, ALU.mult))
                    for m in (15, 13, 11, 9, 7, 5, 3):
                        chain(dve.scalar_tensor_tensor(d[1], d[1], 1.0 / m, d[0], ALU.add, ALU.mult))
                    chain(dve.scalar_tensor_tensor(d[1], d[1], 1.0, d[2], ALU.add, ALU.mult))
                    dtf = dt[:].rearrange("p c r -> p (c r)")
                    dve.scalar_tensor_tensor(dtf, d[1], 2.0, d[4], ALU.mult, ALU.add).then_inc(dt_ready, 1)
                    dve.wait_ge(dt_ready, 1)
                    dve.wait_ge(ea_ready, 1)
                    ea = e_a[:, None, :].broadcast_to([P, NS, R])
                    chain(dve.scalar_tensor_tensor(dA[:], dt[:], -1.0, ea, ALU.mult, ALU.mult))
                    dve.tensor_copy(dA_hi[:], dA[:]).then_inc(dA_ready, 1)
                    dve.wait_ge(dA_ready, 1)
                    dve.tensor_tensor(dA_lo[:], dA[:], dA_hi[:].bitcast(F32), ALU.subtract).then_inc(dA_ready, 1)
                if t >= 20 and t % 2 == 0:
                    j = (t - 20) // 2
                    bank = wait_full(dve, ("cb", j))
                    if j:
                        dve.wait_ge(lm_ready, j)
                    ins = dve.tensor_tensor(cbm[:], bank[:, 0:P], upper[:], ALU.mult)
                    freed(ins, ("cb", j))
                    wait_free(dve, ("cb", j))
                    for i in range(2):
                        wait_free(dve, ("seg", j, i))
                    dve.tensor_tensor(lm[:], lm[:], cbm[:, None, :].broadcast_to([P, RG, P]), ALU.mult
                                      ).then_inc(lm_ready, 1)
                if t >= 21 and t % 2 == 1:
                    j = (t - 21) // 2
                    g, c = divmod(j, 4)
                    yv = y[:, c, 512 * g:512 * g + 512]
                    term = xs_t[:, 0, :]
                    heads = slice(g * RG, g * RG + RG)
                    diag = wait_full(dve, ("diag", j))
                    dve.wait_ge(xsd_ready, j + 1)
                    if c:
                        off = wait_full(dve, ("off", j))
                        ins = dve.tensor_tensor(
                            term.rearrange("p (r d) -> p r d", r=RG), off.rearrange("p (r d) -> p r d", r=RG),
                            decay[:, 0, c, heads][:, :, None].broadcast_to([P, RG, HD]), ALU.mult)
                        freed(ins, ("off", j))
                        wait_free(dve, ("off", j))
                        ssd(dve.tensor_tensor(term, term, yv, ALU.add))
                        ins = dve.tensor_tensor(yv, diag, term, ALU.add)
                    else:
                        ins = dve.tensor_tensor(yv, diag, yv, ALU.add)
                    freed(ins, ("diag", j))
                    if c < 3:
                        new = wait_full(dve, ("state", j))
                        if c:
                            cv = carry[:].rearrange("p (r d) -> p r d", r=RG)
                            ssd(dve.tensor_tensor(cv, cv, decay[:, 2, c, heads][:, :, None].broadcast_to([P, RG, HD]),
                                                  ALU.mult))
                            ins = dve.tensor_tensor(carry[:], new, carry[:], ALU.add)
                        else:
                            ins = dve.tensor_copy(carry[:], new)
                        freed(ins, ("state", j))
                        wait_free(dve, ("state", j))
                if t == 32:
                    dve.wait_ge(m_rms_ready, 1)
                    dve.reciprocal(m_rstd[:, 0:4], m_rms[:, 0:4]).then_inc(m_rstd_ready, 1)
                    dve.wait_ge(m_rstd_ready, 1)
                    dve.wait_ge(gain_landed[0], 32)
                    for i in range(NS):
                        dve.scalar_tensor_tensor(h[:, i, :], h[:, i, :], m_rstd[:, i:i + 1], gain[:, 0, :],
                                                 ALU.mult, ALU.mult).then_inc(ya_norm, 1)
                if X <= b < U:
                    i = t - 4 * X
                    dve.wait_ge(conv_begun, i + 1)
                    for k in range(1, 4):
                        w = cols[:, 12 * (3 - k) + i:12 * (3 - k) + i + 1]
                        dst = conv[:, i % 2, k:SEQ]
                        ins = dve.scalar_tensor_tensor(dst, acc[:, s, 0:SEQ - k], w, dst, ALU.mult, ALU.add)
                        if k < 3:
                            ins.then_inc(conv_step, 1)
                            dve.wait_ge(conv_step, 2 * i + k)
                        else:
                            ins.then_inc(dve_evac, 1)
                elif U <= b < Z:
                    i = t - 4 * U
                    dve.wait_ge(*emptied(b, s))
                    if i == 0 or i == 4:
                        for head in range(4 * (i // 4), 4 * (i // 4) + 4):
                            wait_free(dve, ("mix", head))
                    c0 = 512 * (b - U)
                    hv = h[:, s, c0:c0 + 512]
                    dve.tensor_tensor(hv, hv, tmp[:, s, :], ALU.mult).then_inc(ya_mul, 1)
                elif b >= Z:
                    g = b - Z
                    dve.wait_ge(*emptied(b, s))
                    wait_free(dve, ("diag", 4 * g + s))
                    yv = y[:, s, 512 * g:512 * g + 512]
                    dve.tensor_tensor(yv, yv, tmp[:, s, :], ALU.mult).then_inc(yb_mul, 1)

            def yb_scale(g):
                at = slice(4 + 4 * g, 8 + 4 * g)
                dve.wait_ge(m_rms_ready, 2 + g)
                dve.reciprocal(m_rstd[:, at], m_rms[:, at]).then_inc(m_rstd_ready, 1)
                dve.wait_ge(m_rstd_ready, 2 + g)
                dve.wait_ge(gain_landed[1], 32)
                for i in range(NS):
                    yv = y[:, i, 512 * g:512 * g + 512]
                    dve.scalar_tensor_tensor(yv, yv, m_rstd[:, 4 + 4 * g + i:5 + 4 * g + i],
                                             gain[:, 1, 512 * g:512 * g + 512], ALU.mult, ALU.mult).then_inc(yb_norm, 1)

            for s in range(NS):
                yt_evac(0, s, s)
            yb_scale(0)
            yb_scale(1)
            for b in range(OUT, OUT + 4):
                for s in range(4):
                    t = 4 * b + s
                    split_lo(b + 1, s)
                    if b == OUT and s == 1:
                        for i in range(NS):
                            yt_evac(1, i, 4 + i)
                        add_group(b, 0)
                    if 41 <= t < 45:
                        for q in range(2):
                            yt_evac(2 + q, t - 41, 8 + 2 * (t - 41) + q)
                    if t == 45:
                        for k in range(2):
                            dve.wait_ge(pt_hi, k + 1)
                            name = ("pt", k)
                            dve.tensor_tensor(p_lo[:, k, :], side[:, fills[name][0], :], p_hi[:, k, :].bitcast(F32),
                                              ALU.subtract).then_inc(side_free[fills[name][0]], 1)
                    if b == OUT + 3 and s >= 2:
                        xt_evac(1, s - 2)
                    if not (b == OUT and s == 0):
                        add_group(b, s)
                    if b == OUT + 3:
                        normed(1, s)

            for s in range(4):
                split_lo(FF, s)
                if s == 0:
                    xt_evac(1, 2)
                if s == 2:
                    xt_evac(1, 3)

            def ff1(b, e, trip=0):
                for s in range(4):
                    n = 4 * e + s
                    split_lo(b + 1, s, trip=trip)
                    dve.wait_ge(act_evac, before[b] + s + 1 + 8 * trip)
                    if not (isinstance(e, int) and n < 2) or not isinstance(trip, int):
                        dve.wait_ge(hid_lo, n - 1 + 8 * trip)
                    dve.tensor_tensor(tmp[:, 2 + s % 2, :], tmp[:, s % 2, :], tmp[:, s % 2, :], ALU.mult
                                      ).then_inc(sq_ready, 1)
                    dve.wait_ge(hid_hi, n + 1 + 8 * trip)
                    k = 4 * (e % 2) + s
                    dve.tensor_tensor(a_lo[:, k, :], tmp[:, 2 + s % 2, :], a_hi[:, k, :].bitcast(F32), ALU.subtract
                                      ).then_inc(hid_lo, 1)

            def ff2(b, trip=0):
                for s in range(4):
                    split_lo(b + 1, s, trip=trip)
                    add_group(b, s, trip=trip)

            ff1(FF, 0)
            with dve.Fori(0, 3) as i:
                for q in range(2):
                    ff1(FF + 1 + 2 * q, 1 + q, i)
                    ff2(FF + 2 + 2 * q, i)
            ff1(LAST - 3, 7)
            ff2(LAST - 2)
            for s in range(4):
                split_lo(GATE, s)
                if s >= 2:
                    xt_evac(2, s - 2)
                add_group(LAST - 1, s)
                normed(2, s)

            for i in range(8):
                b, s = GATE + i // 4, i % 4
                if b == GATE:
                    split_lo(GATE + 1, s)
                if i == 0:
                    xt_evac(2, 2)
                if i == 2:
                    xt_evac(2, 3)
                at = slice(512 * (i // 4), 512 * (i // 4) + 512)
                dve.wait_ge(*emptied(b, s))
                dve.tensor_tensor(y[:, s, at], y[:, s, at], conv[:, i % 2, :], ALU.mult).then_inc(gated, 1)
                dve.wait_ge(gated, i + 1)
                dve.tensor_tensor(h[:, s, at], h[:, s, at], y[:, s, at], ALU.add).then_inc(h_final, 1)
                if b > GATE:
                    normed(3, s)

        @block.tensor
        def _(pe):
            def banks_free(b, s, trip=None):
                if b == 0:
                    return
                c, r = last_user(b, s)
                signal, value = emptied(c, r)
                pe.wait_ge(signal, value if trip is None else value + 8 * trip)
                if trip is not None and b == FF + 1:
                    signal, value = emptied(FF + 4, 2 + s // 2)
                    pe.wait_ge(signal, value - 8 + 8 * trip)

            def split_ready(b, p, trip=0):
                pe.wait_ge(lo_ready, 4 * b + p + 1 + 16 * trip)

            def product(dst, st, mv, start, stop):
                pe.matmul(dst, st[0], mv[0], start=start, stop=False)
                pe.matmul(dst, st[0], mv[1], start=False, stop=False)
                return pe.matmul(dst, st[1], mv[0], start=False, stop=stop)

            def group_rows(b, s, act_hl, signal=True):
                banks_free(b, s)
                for k in range(KT):
                    if s == 0 and k % 2 == 0:
                        split_ready(b, k // 2)
                    at = (slice(None), k, slice(s * P, s * P + P))
                    ins = product(acc[:, s, :], [t[at] for t in act_hl],
                                  [t[:, b % 2, k, :] for t in (w_hi, w_lo)], k == 0, k == KT - 1)
                ins.then_inc(acc_full, 1)

            def group_cols(b, s, act_hl, trip=None):
                banks_free(b, s, trip)
                for k in range(KT):
                    if s == 0 and k % 2 == 0:
                        split_ready(b, k // 2, 0 if trip is None else trip)
                    ins = product(acc[:, s, :], [t[:, b % 2, k, s * P:s * P + P] for t in (w_hi, w_lo)],
                                  [t[:, k, :] for t in act_hl], k == 0, k == KT - 1)
                ins.then_inc(acc_full, 1)

            def group_pair(b, s, act_hl, k0, trip=None, nk=4):
                banks_free(b, s, trip)
                for n in range(2):
                    for k in range(nk):
                        if s == 0 and n == 0 and nk == 4:
                            split_ready(b, k, 0 if trip is None else trip)
                        elif s == 0 and nk == 2:
                            split_ready(b, 2 * k + n)
                        sub = 2 * k + n if nk == 4 else 2 * (2 * k + n)
                        at = (slice(None), k0 + k, slice(s * P, s * P + P))
                        ins = product(acc[:, 2 * (s % 2) + n, :], [t[at] for t in act_hl],
                                      [t[:, b % 2, sub, :] for t in (w_hi, w_lo)], k == 0, k == nk - 1)
                ins.then_inc(acc_full, 1)

            def open_bank(name):
                bank, n = fills[name]
                if n:
                    pe.wait_ge(side_free[bank], n)
                return side[:, bank, :]

            def filled(ins, name):
                ins.then_inc(side_full[fills[name][0]], 1)

            def turn(name, src, k0=0):
                bank = open_bank(name)
                for i in range(4):
                    ins = pe.transpose(bank[:, i * P:i * P + P], src(i), ident[:])
                filled(ins, name)

            def turn_norm(n, s):
                pe.wait_ge(xn_ready, 4 * n + s + 1)
                src = h[:, s, :] if n == 0 else tmp[:, 2 * (s % 2):2 * (s % 2) + 2, :].rearrange("p a n -> p (a n)")
                for q in range(2):
                    turn(("xt", n, s, q), lambda i: src[:, (4 * q + i) * P:(4 * q + i + 1) * P])

            A, B = (a_hi, a_lo), (b_hi, b_lo)

            pe.wait_ge(consts_ready, 3)
            pe.wait_ge(rows_landed, 16 * 3)
            filled(pe.transpose(open_bank("cols")[:, 0:68], rows[0:68, :], ident[0:68, 0:68]), "cols")
            for s in range(NS):
                turn_norm(0, s)

            for t in range(4 * OUT):
                b, s = divmod(t, 4)
                if b == 0:
                    for q in range(2):
                        wait_free(pe, ("xt", 0, s, q))
                if X <= b < U:
                    group_cols(b, s, A)
                else:
                    group_rows(b, s, A)
                if t == 0:
                    pe.wait_ge(ws_landed, 16)
                    for i in range(2):
                        turn(("ws", i), lambda g: y[:, 0, (4 * i + g) * P:(4 * i + g + 1) * P])
                if 9 <= t < 17:
                    i = t - 9
                    pe.wait_ge(silu_done, i + 1)
                    turn(("xs", i), lambda c: xs_t[:, i % 2, c * P:c * P + P])
                if t == 10:
                    bank = open_bank("dt")
                    pe.wait_ge(wdt_ready, 2)
                    for k in range(KT):
                        ins = product(bank, [w[:, k, :] for w in (seg_hi, seg_lo)], [x[:, k, :] for x in A],
                                      k == 0, k == KT - 1)
                    filled(ins, "dt")
                if t == 11:
                    bank = open_bank("dt_nat")
                    wait_free(pe, "dt")
                    for c in range(NS):
                        ins = pe.transpose(bank[:, c * R:c * R + R], dtT[:, c * P:c * P + P], ident[0:R, 0:R])
                    filled(ins, "dt_nat")
                if t == 13:
                    bank = open_bank("decay")
                    pe.wait_ge(dA_ready, 2)
                    for i, m in enumerate((upper, after, ones)):
                        ins = pe.matmul(bank[:, i * NS * R:(i + 1) * NS * R], m[:],
                                        dA[:].rearrange("p c r -> p (c r)"), start=True, stop=True)
                    filled(ins, "decay")
                if 14 <= t < 18:
                    if t == 14:
                        pe.wait_ge(v_ready, NS)
                        wait_free(pe, ("ws", 1))
                    for i in range(2):
                        g = 2 * (t - 14) + i
                        bank = open_bank(("mix", g))
                        filled(pe.matmul(bank.rearrange("p (c n) -> p c n", c=NS), wsT[:, g, :],
                                         h[:, :, g * P:g * P + P], start=True, stop=True), ("mix", g))
                if 17 <= t < 19:
                    g = t - 17
                    pe.wait_ge(silu_done, 9 + g)
                    turn(("b_nat", g), lambda c: bcT[:, g, c * P:c * P + P])
                if t >= 19 and t % 2 == 1 and t < 35:
                    j = (t - 19) // 2
                    g, c = divmod(j, 4)
                    at = slice(c * P, c * P + P)
                    bank = open_bank(("cb", j))
                    if j % 4 == 0:
                        pe.wait_ge(silu_done, 11 + g)
                    filled(pe.matmul(bank[:, 0:P], bcT[:, g, at], bcT[:, 2 + g, at], start=True, stop=True), ("cb", j))
                    pe.wait_ge(seg_ready, 2 * j + 2)
                    if j == 0:
                        pe.wait_ge(after_ready, 1)
                    for i in range(2):
                        bank = open_bank(("seg", j, i))
                        for k, m in enumerate((seg_hi, seg_lo)):
                            ins = pe.matmul(bank, after_r[:], m[:, 4 * i:4 * i + 4, :].rearrange("p r n -> p (r n)"),
                                            start=(k == 0), stop=(k == 1))
                        filled(ins, ("seg", j, i))
                if t >= 20 and t % 2 == 0:
                    j = (t - 20) // 2
                    g, c = divmod(j, 4)
                    at = slice(c * P, c * P + P)
                    if c:
                        bank = open_bank(("off", j))
                        wait_free(pe, ("state", j - 1))
                        filled(pe.matmul(bank, bcT[:, 2 + g, at], carry[:], start=True, stop=True), ("off", j))
                    pe.wait_ge(xdt_ready, 2 * j + 2)
                    bank = open_bank(("diag", j))
                    pe.wait_ge(lm_ready, j + 1)
                    for r in range(RG):
                        ins = pe.matmul(bank[:, r * HD:r * HD + HD], lm[:, r, :], xdt[:, r * HD:r * HD + HD],
                                        start=True, stop=True)
                    filled(ins, ("diag", j))
                    if c < 3:
                        bank = open_bank(("state", j))
                        if j == 0:
                            for i in range(2):
                                wait_free(pe, ("b_nat", i))
                        filled(pe.matmul(bank, b_nat[:, g, c, :], xdd[:], start=True, stop=True), ("state", j))

            pe.wait_ge(ya_norm, NS)
            for s in range(NS):
                turn(("yt", 0, s), lambda i: h[:, s, i * P:i * P + P])
            for b in range(OUT, OUT + 4):
                for s in range(4):
                    t = 4 * b + s
                    if b < OUT + 2:
                        wait_free(pe, ("yt", b - OUT, s))
                    elif b == OUT + 2:
                        for q in range(2):
                            wait_free(pe, ("yt", 2 + q, s))
                    group_pair(b, s, A if b < OUT + 2 else B, 4 * ((b - OUT) % 2))
                    if b == OUT and s == 0:
                        for i in range(NS):
                            turn(("yt", 1, i), lambda k: h[:, i, (4 + k) * P:(5 + k) * P])
                    if 40 <= t < 44:
                        i = t - 40
                        pe.wait_ge(yb_norm, 5 + i)
                        for q in range(2):
                            turn(("yt", 2 + q, i), lambda k: y[:, i, (4 * q + k) * P:(4 * q + k + 1) * P])
                    if t == 44:
                        pe.wait_ge(p_landed, 16)
                        for q in range(2):
                            turn(("pt", q), lambda i: tmp[:, i // 2, 256 * (i % 2) + q * P:256 * (i % 2) + (q + 1) * P])
                    if b == OUT + 3 and s:
                        turn_norm(1, s - 1)

            for k in range(2):
                wait_free(pe, ("pt", k))
            for s in range(4):
                group_pair(PLE, s, (p_hi, p_lo), 0, nk=2)
                if s == 1:
                    turn_norm(1, 3)

            def ff1(b, trip=None):
                for s in range(4):
                    group_cols(b, s, B, trip)

            def ff2(b, e, trip=None):
                for s in range(4):
                    if s == 0:
                        pe.wait_ge(hid_lo, 4 * e + 4 + (0 if trip is None else 8 * trip))
                    group_pair(b, s, A, 4 * (e % 2), trip)

            for s in range(NS):
                for q in range(2):
                    wait_free(pe, ("xt", 1, s, q))
            ff1(FF)
            with pe.Fori(0, 3) as i:
                for q in range(2):
                    ff1(FF + 1 + 2 * q, i)
                    ff2(FF + 2 + 2 * q, q, i)
            ff1(LAST - 3)
            ff2(LAST - 2, 6)
            for s in range(4):
                if s == 0:
                    pe.wait_ge(hid_lo, 4 * NE)
                group_pair(LAST - 1, s, A, 4)
                if s:
                    turn_norm(2, s - 1)

            for i in range(8):
                b, s = GATE + i // 4, i % 4
                if b == GATE:
                    for q in range(2):
                        wait_free(pe, ("xt", 2, s, q))
                group_rows(b, s, B)
                if i == 1:
                    turn_norm(2, 3)


_INS = ["x", "p", "norm_mix_g", "w_in", "gm_v_norm_g", "gm_ws", "gm_bs", "gm_out_norm_g", "ssd_conv_w", "ssd_conv_b",
        "ssd_dt_bias", "ssd_a_log", "ssd_d", "ssd_norm_g", "w_out", "norm_mlp_g", "w_ff1", "w_ff2", "ple_norm_g",
        "w_ple_gate", "w_ple_proj", "final_norm_g"]


def kernel(**inputs):
    import numpy as np
    import concourse.bacc as bacc
    from concourse.bass_utils import run_bass_kernel_spmd

    nc = bacc.Bacc("TRN2", target_bir_lowering=False, num_devices=1)
    arrays, aps = {}, {}
    for name in _INS:
        arr = np.ascontiguousarray(inputs[name])
        arrays[f"in_{name}"] = arr
        aps[name] = nc.dram_tensor(f"in_{name}", arr.shape, mybir.dt.from_np(arr.dtype), kind="ExternalInput").ap()
    shape = inputs["x"].shape
    out = nc.dram_tensor("out_0", shape, F32, kind="ExternalOutput").ap()
    build_layer(nc, aps, out)
    r = run_bass_kernel_spmd(nc, [arrays], core_ids=[0])
    return r.results[0]["out_0"]
```

```python
from contextlib import ExitStack

import concourse.bass as bass
from concourse import mybir

P = 128
F32 = mybir.dt.float32
F32R = mybir.dt.float32r
ALU = mybir.AluOpType
ACT = mybir.ActivationFunctionType
AX = mybir.AxisListType

V, X, BC, U, Z, OUT, PLE, FF, GATE = 0, 2, 4, 5, 7, 9, 13, 14, 30
EPS = 1e-6
WARM = 10
OUT_DVE = 640


def build_layer(nc, a, out):
    _, SEQ, D = a["x"].shape
    NS = SEQ // P
    KT = D // P
    W = a["gm_v_norm_g"].shape[1]
    GH = a["gm_ws"].shape[1]
    R = a["ssd_a_log"].shape[1]
    G2 = 2
    RG = R // G2
    HD = W // R
    DF = a["w_ff1"].shape[2]
    NE = DF // 512
    assert (NS, KT, W, GH, RG, HD, NE) == (4, 8, 1024, 8, 8, 64, 8)
    LAST = FF + 2 * NE
    assert LAST == GATE

    w_in = a["w_in"][0].rearrange("(k p) n -> p k n", p=P)
    w_out = a["w_out"][0].rearrange("(k p) n -> p k n", p=P)
    w_ff1 = a["w_ff1"][0].rearrange("(k p) n -> p k n", p=P)
    w_ff2 = a["w_ff2"][0].rearrange("(k p) n -> p k n", p=P)
    w_gate = a["w_ple_gate"][0].rearrange("(k p) n -> p k n", p=P)
    w_ple = a["w_ple_proj"][0].rearrange("(k p) n -> p k n", p=P)
    x_dram = a["x"][0].rearrange("(s p) n -> p s n", p=P)
    out_dram = out[0].rearrange("(s p) n -> p s n", p=P)
    p_dram = a["p"][0, 0].rearrange("(s p) n -> p s n", p=P)

    with ExitStack() as ctx:
        def sb(name, shape, dt=F32, where=ctx):
            return where.enter_context(nc.sbuf_tensor(name, shape, dt))

        def sem(name):
            return ctx.enter_context(nc.semaphore(name))

        w_raw = sb("w_raw", [P, 4, 2, 512])
        w_hi = sb("w_hi", [P, 2, 8, 512], F32R)
        w_lo = sb("w_lo", [P, 2, 8, 512], F32R)
        a_hi = sb("a_hi", [P, KT, SEQ], F32R)
        a_lo = sb("a_lo", [P, KT, SEQ], F32R)
        h = sb("h", [P, NS, D])
        y = sb("y", [P, NS, D])
        gain = sb("gain", [P, 2, D])
        tmp = sb("tmp", [P, 4, 512])
        ident = sb("ident", [P, P])
        upper = sb("upper", [P, P])
        after = sb("after", [P, P])
        ones = sb("ones", [P, P])
        eps = sb("eps", [P, 1])
        rows = sb("rows", [P, P])
        cols = sb("cols", [P, 68])
        a_log = sb("a_log", [P, R])
        d_skip = sb("d_skip", [P, R])
        dt_b = sb("dt_b", [2 * R, 1])
        w_dt = sb("w_dt", [P, KT, R])
        dt = sb("dt", [P, NS, R])
        e_a = sb("e_a", [P, R])
        dA = sb("dA", [P, NS, R])
        cs = sb("cs", [P, NS * R])
        csT = sb("csT", [NS * R, P])
        decay = sb("decay", [P, 3, NS, R])
        f_ssq = sb("f_ssq", [P, 8])
        f_base = sb("f_base", [P, NS])
        f_rms = sb("f_rms", [P, NS])
        f_rstd = sb("f_rstd", [P, NS])
        ssq = sb("ssq", [P, 12])
        rms = sb("rms", [P, 12])
        early_rms = sb("early_rms", [P, 1])
        rstd = sb("rstd", [P, 12])
        v_ssq = sb("v_ssq", [P, NS, GH])
        v_rms = sb("v_rms", [P, NS, GH])
        v_rstd = sb("v_rstd", [P, NS, GH])
        m_ssq = sb("m_ssq", [P, 12])
        m_rms = sb("m_rms", [P, 12])
        m_rstd = sb("m_rstd", [P, 12])
        with ExitStack() as early:
            conv = sb("conv", [P, 2, 512], where=early)
            xs_t = sb("xs_t", [P, 2, 512], where=early)
        p_hi = sb("p_hi", [P, 2, SEQ], F32R)
        p_lo = sb("p_lo", [P, 2, SEQ], F32R)
        with ExitStack() as early:
            with ExitStack() as first:
                dtT = sb("dtT", [2 * R, SEQ], where=first)
                dts = sb("dts", [P, 5, NS * R], where=first)
            lm = sb("lm", [P, RG, P], where=early)
            cbm = sb("cbm", [P, P], where=early)
            bcT = sb("bcT", [P, 4, SEQ], where=early)
            with ExitStack() as first:
                wsT = sb("wsT", [P, GH, P], where=first)
            b_nat = sb("b_nat", [P, G2, NS, P], where=early)
            xdt = sb("xdt", [P, 512], where=early)
            xdd = sb("xdd", [P, 512], where=early)
            with ExitStack() as first:
                wdt_hl = sb("wdt_hl", [P, KT, P], F32R, where=first)
                wdt_h = sb("wdt_h", [P, KT, P], F32R, where=first)
            seg = sb("seg", [P, 2, RG, P], where=early)
            carry = sb("carry", [P, 512], where=early)
        b_hi = sb("b_hi", [P, KT, SEQ], F32R)
        b_lo = sb("b_lo", [P, KT, SEQ], F32R)

        acc = ctx.enter_context(nc.psum_tensor("acc", [P, 4, 512], F32))
        side = ctx.enter_context(nc.psum_tensor("side", [P, 4, 512], F32))

        cs_dram = nc.dram_tensor("cs_dram", [NS * R, P], F32, kind="Internal").ap()

        w_landed = [sem(f"w_landed{i}") for i in range(4)]
        hi_ready = sem("hi_ready")
        lo_ready = sem("lo_ready")
        acc_full = sem("acc_full")
        act_evac = sem("act_evac")
        dve_evac = sem("dve_evac")
        side_full = [sem(f"side_full{i}") for i in range(4)]
        side_free = [sem(f"side_free{i}") for i in range(4)]
        x_landed = [sem(f"x_landed{i}") for i in range(NS)]
        gain_landed = [sem(f"gain_landed{i}") for i in range(2)]
        rows_landed, small_landed = sem("rows_landed"), sem("small_landed")
        ws_landed = sem("ws_landed")
        p_landed = sem("p_landed")
        ssq_ready, rms_ready = sem("ssq_ready"), sem("rms_ready")
        rstd_ready, xn_ready = sem("rstd_ready"), sem("xn_ready")
        xt_hi = sem("xt_hi")
        consts_ready = sem("consts_ready")
        eps_ready = sem("eps_ready")
        sqrt_loaded = sem("sqrt_loaded")
        dtb_zero = sem("dtb_zero")
        v_sq, v_sum = sem("v_sq"), sem("v_sum")
        v_rms_ready, v_rstd_ready = sem("v_rms_ready"), sem("v_rstd_ready")
        v_scaled, v_ready = sem("v_scaled"), sem("v_ready")
        conv_begun, silu_done = sem("conv_begun"), sem("silu_done")
        conv_step = sem("conv_step")
        wdt_zero, wdt_ready = sem("wdt_zero"), sem("wdt_ready")
        dt_step, dt_exp = sem("dt_step"), sem("dt_exp")
        ea_ready, dt_ready, dA_ready = sem("ea_ready"), sem("dt_ready"), sem("dA_ready")
        cs_ready, cs_stored = sem("cs_ready"), sem("cs_stored")
        seg_landed = [sem(f"seg_landed{i}") for i in range(2)]
        seg_step, seg_ready, xdt_ready, xsd_ready = sem("seg_step"), sem("seg_ready"), sem("xdt_ready"), sem("xsd_ready")
        exp_done, lm_ready = sem("exp_done"), sem("lm_ready")
        ssd_step = sem("ssd_step")
        ya_mul, yb_mul = sem("ya_mul"), sem("yb_mul")
        m_ssq_ready, m_rms_ready = sem("m_ssq_ready"), sem("m_rms_ready")
        m_rstd_ready = sem("m_rstd_ready")
        ya_norm, yb_norm = sem("ya_norm"), sem("yb_norm")
        yt_hi, pt_hi = sem("yt_hi"), sem("pt_hi")
        sq_ready, hid_hi, hid_lo = sem("sq_ready"), sem("hid_hi"), sem("hid_lo")
        gated, h_final, h_gain = sem("gated"), sem("h_final"), sem("h_gain")
        f_ssq_ready, f_base_ready, f_rms_ready = sem("f_ssq_ready"), sem("f_base_ready"), sem("f_rms_ready")
        f_rstd_ready = sem("f_rstd_ready")
        out_act, out_dve = sem("out_act"), sem("out_dve")
        out_done = sem("out_done")

        kind = {}
        for b in range(GATE + 2):
            if b in (OUT, OUT + 1, OUT + 2, OUT + 3):
                kind[b] = "pair_dve"
            elif b == PLE:
                kind[b] = "pair_act"
            elif FF <= b < GATE:
                kind[b] = "pair_dve" if b == GATE - 1 or (b > FF and (b - FF) % 2 == 0) else "one_act"
            elif X <= b < U:
                kind[b] = "one_dve"
            else:
                kind[b] = "one_act"
        before = {b: 4 * sum(kind[c][-3:] == kind[b][-3:] for c in range(b)) for b in kind}

        def emptied(b, s, shift=0):
            return (act_evac if kind[b].endswith("act") else dve_evac), before[b] + s + 1 + shift

        def last_user(b, s):
            pair, prev = kind[b].startswith("pair"), kind[b - 1].startswith("pair") if b else False
            if pair:
                if s >= 2:
                    return b, s - 2
                return b - 1, (s + 2 if prev else 2 * s + 1)
            return b - 1, (2 + s // 2 if prev else s)

        plan = [(("xt", 0, s, q), (2 * s + q) % 4) for s in range(NS) for q in range(2)]
        plan += [("cols", 2)]
        plan += [(("ws", i), i) for i in range(2)]
        for t in range(9, 20):
            if t < 17:
                plan.append((("xs", t - 9), (t - 9) % 2))
            if t == 10:
                plan.append(("dt", 2))
            if t == 11:
                plan.append(("dt_nat", 3))
            if t == 16:
                plan.append(("csT", 0))
            if 15 <= t < 19:
                plan += [(("mix", 2 * (t - 15) + i), 2 + i) for i in range(2)]
            if t == 15:
                plan.append(("decay", 1))
            if t >= 18:
                plan.append((("b_nat", t - 18), 1))
        for j in range(8):
            plan.append((("cb", j), 3))
            if j % 4 > 0:
                plan.append((("off", j), 3))
            plan.append((("diag", j), 2 - j % 2))
            if j % 4 < 3:
                plan.append((("state", j), 0))
        plan += [(("yt", 0, s), (0, 2, 3, 0)[s]) for s in range(NS)]
        plan += [(("yt", 1, s), (s + 1) % 4) for s in range(NS)]
        plan += [(("yt", 2 + q, s), (2 * s + q) % 4) for s in range(NS) for q in range(2)]
        plan += [(("pt", k), k) for k in range(2)]
        plan += [(("xt", n, s, q), (2 * s + q) % 4) for n in (1, 2) for s in range(NS) for q in range(2)]
        fills, order = {}, [0] * 4
        for name, bank in plan:
            fills[name] = (bank, order[bank])
            order[bank] += 1

        def wait_full(eng, name):
            bank, n = fills[name]
            eng.wait_ge(side_full[bank], n + 1)
            return side[:, bank, :]

        def wait_filled(eng, name):
            bank, n = fills[name]
            eng.wait_ge(side_full[bank], n + 1)

        def wait_free(eng, name):
            bank, n = fills[name]
            eng.wait_ge(side_free[bank], n + 1)

        def freed(ins, name):
            ins.then_inc(side_free[fills[name][0]], 1)

        block = ctx.enter_context(nc.Block())

        @block.sync
        def _(sp):
            def piece(b, p, src, dst, shift=0):
                if not (isinstance(b, int) and b == 0):
                    sp.wait_ge(lo_ready, 4 * (b - 1) + p + 1 + shift)
                sp.dma_start(dst, src).then_inc(w_landed[p], 16)

            def load_k(b, w, c0, shift=0):
                for p in range(4):
                    piece(b, p, w[:, 2 * p:2 * p + 2, bass.ds(c0, 512)], w_raw[:, p], shift)

            def load_rows(b, w, k0, shift=0):
                for p in range(4):
                    piece(b, p, w[:, bass.ds(k0 + p, 1), :],
                          w_raw[:, p].rearrange("p a n -> p (a n)")[:, None, :], shift)

            def load_gain(g, slot):
                sp.dma_start(gain[:, slot, :], g.partition_broadcast(P)).then_inc(gain_landed[slot], 16)

            def load_x(s):
                sp.dma_start(h[:, s, :], x_dram[:, s, :]).then_inc(x_landed[s], 16)

            def first_piece(p):
                piece(0, p, w_in[:, 2 * p:2 * p + 2, W:W + 512], w_raw[:, p])

            load_x(0)
            load_gain(a["norm_mix_g"][0], 0)
            for p in range(3):
                first_piece(p)
            load_x(1)
            first_piece(3)
            load_x(2)
            load_x(3)
            load_k(V + 1, w_in, W + 512)
            cw = a["ssd_conv_w"][0].rearrange("k (i p) -> (k i) p", p=P)
            sp.dma_start(rows[0:48, :], cw).then_inc(rows_landed, 16)
            sp.dma_start(rows[48:60, :], a["ssd_conv_b"][0].rearrange("(i p) -> i p", p=P)).then_inc(rows_landed, 16)
            sp.dma_start(rows[60:68, :], a["gm_bs"][0]).then_inc(rows_landed, 16)
            sp.dma_start(y[:, 0:1, :].rearrange("p a (g s) -> p (a g) s", g=GH),
                         a["gm_ws"][0].rearrange("g t s -> t g s")).then_inc(ws_landed, 16)
            sp.dma_start(a_log[:], a["ssd_a_log"][0].partition_broadcast(P)).then_inc(small_landed, 16)
            sp.dma_start(d_skip[:], a["ssd_d"][0].partition_broadcast(P)).then_inc(small_landed, 16)
            sp.wait_ge(dtb_zero, 1)
            sp.dma_start(dt_b[0:R, :], a["ssd_dt_bias"][0].rearrange("(p o) -> p o", o=1)).then_inc(small_landed, 16)
            sp.dma_start(w_dt[:], w_in[:, :, 4 * W + 512:4 * W + 512 + R]).then_inc(small_landed, 16)
            load_gain(a["gm_v_norm_g"][0], 1)
            for i in range(3):
                load_k(X + i, w_in, 3 * W + 512 * i)
            sp.wait_ge(xn_ready, NS)
            load_gain(a["gm_out_norm_g"][0], 0)
            load_k(U, w_in, 0)
            sp.wait_ge(v_ready, NS)
            load_gain(a["ssd_norm_g"][0], 1)
            load_k(U + 1, w_in, 512)
            for i in range(2):
                load_k(Z + i, w_in, 2 * W + 512 * i)
            load_rows(OUT, w_out, 0)
            sp.wait_ge(ya_norm, NS)
            load_gain(a["norm_mlp_g"][0], 0)
            load_rows(OUT + 1, w_out, 4)
            for s in range(NS):
                wait_filled(sp, ("yt", 1, s))
                sp.dma_start(h[:, s, :], x_dram[:, s, :]).then_inc(x_landed[s], 16)
            load_rows(OUT + 2, w_out, 8)
            sp.wait_ge(yb_mul, 8)
            sp.dma_start(tmp[:, 0:2, :].rearrange("p a (b n) -> p (a b) n", b=2), p_dram).then_inc(p_landed, 16)
            load_rows(OUT + 3, w_out, 12)
            sp.wait_ge(yb_norm, 8)
            load_gain(a["ple_norm_g"][0], 1)
            for p in range(4):
                piece(PLE, p, w_ple[:, p // 2, 512 * (p % 2):512 * (p % 2) + 512], w_raw[:, p, 0, :])
            load_k(FF, w_ff1, 0)
            with sp.Fori(0, 3) as i:
                b = FF + 1
                for q in range(2):
                    load_k(b + 2 * q, w_ff1, i * 1024 + 512 * (q + 1), 16 * i)
                    load_rows(b + 2 * q + 1, w_ff2, i * 8 + 4 * q, 16 * i)
            load_k(LAST - 3, w_ff1, 7 * 512)
            load_rows(LAST - 2, w_ff2, 6 * 4)
            load_rows(LAST - 1, w_ff2, 7 * 4)
            sp.wait_ge(xn_ready, 2 * NS)
            load_gain(a["final_norm_g"], 0)
            for i in range(2):
                load_k(GATE + i, w_gate, 512 * i)
            for s in range(NS):
                sp.wait_ge(out_dve, s + 1)
                if s == NS - 1:
                    sp.wait_ge(out_act, 1)
                sp.dma_start(out_dram[:, s, :], y[:, s, :]).then_inc(out_done, 16)
            sp.wait_ge(out_done, 16 * NS)

        @block.gpsimd
        def _(pool):
            pool.memset(ident[:], 0.0).then_inc(consts_ready, 1)
            pool.memset(ones[:], 1.0).then_inc(consts_ready, 1)
            pool.wait_ge(consts_ready, 2)
            pool.affine_select(out=ident[:], in_=ident[:], compare_op=ALU.not_equal, fill=1.0, base=0,
                               pattern=[[-1, P]], channel_multiplier=1).then_inc(consts_ready, 1)
            pool.affine_select(out=upper[:], in_=ones[:], compare_op=ALU.is_ge, fill=0.0, base=0,
                               pattern=[[1, P]], channel_multiplier=-1).then_inc(consts_ready, 1)
            pool.affine_select(out=after[:], in_=ones[:], compare_op=ALU.is_ge, fill=0.0, base=-1,
                               pattern=[[-1, P]], channel_multiplier=1).then_inc(consts_ready, 1)
            pool.memset(dt_b[:], 0.0).then_inc(dtb_zero, 1)
            for t in (wdt_hl, wdt_h):
                pool.memset(t[:].bitcast(F32), 0.0).then_inc(wdt_zero, 1)
            for s in range(NS):
                pool.wait_ge(act_evac, 4 + s + 1)
                if s < 2:
                    pool.wait_ge(xn_ready, 3 + s)
                else:
                    pool.wait_ge(v_sum, s - 1)
                pool.tensor_tensor(tmp[:, 2 * (s % 2):2 * (s % 2) + 2, :].rearrange("p a n -> p (a n)"),
                                   h[:, s, :], h[:, s, :], ALU.mult).then_inc(v_sq, 1)
            for s in range(NS):
                if s == 0:
                    pool.wait_ge(gain_landed[1], 16)
                pool.wait_ge(v_scaled, s + 1)
                pool.tensor_tensor(h[:, s, :], h[:, s, :], gain[:, 1, :], ALU.mult).then_inc(v_ready, 1)
            pool.wait_ge(cs_ready, 1)
            for j in range(8):
                g, c = divmod(j, 4)
                heads = slice(g * RG, g * RG + RG)
                sg = seg[:, j % 2]
                pool.wait_ge(seg_landed[j % 2], 16 * (j // 2 + 1))
                pool.tensor_tensor(sg, sg, cs[:, c * R + g * RG:c * R + (g + 1) * RG][:, :, None].broadcast_to(
                    [P, RG, P]), ALU.subtract).then_inc(seg_step, 1)
                pool.wait_ge(seg_step, j + 1)
                pool.tensor_tensor(sg, sg, upper[:, None, :].broadcast_to([P, RG, P]), ALU.mult
                                   ).then_inc(seg_ready, 1)
                if j == 0:
                    for i in range(8):
                        wait_free(pool, ("xs", i))
                    wait_free(pool, "decay")
                else:
                    wait_filled(pool, ("diag", j - 1))
                    if (j - 1) % 4 < 3:
                        wait_filled(pool, ("state", j - 1))
                xs = y[:, c, 512 * g:512 * g + 512].rearrange("p (r d) -> p r d", r=RG)
                xdt_v, xdd_v = (t[:].rearrange("p (r d) -> p r d", r=RG) for t in (xdt, xdd))
                pool.tensor_tensor(xdt_v, xs, dt[:, c, heads][:, :, None].broadcast_to([P, RG, HD]),
                                   ALU.mult).then_inc(xdt_ready, 1)
                pool.wait_ge(xdt_ready, 2 * j + 1)
                pool.tensor_tensor(xdd_v, xdt_v, decay[:, 1, c, heads][:, :, None].broadcast_to([P, RG, HD]),
                                   ALU.mult).then_inc(xdt_ready, 1)
                if j == 0:
                    pool.wait_ge(small_landed, 16 * 4)
                pool.tensor_tensor(xs, xs, d_skip[:, heads][:, :, None].broadcast_to([P, RG, HD]),
                                   ALU.mult).then_inc(xsd_ready, 1)

        @block.scalar
        def _(act):
            def split_hi(b, p, shift=0, trip=0):
                half = b % 2
                act.wait_ge(w_landed[p], 16 * (b + 1) + 64 * trip)
                if b >= 2:
                    act.wait_ge(acc_full, 4 * (b - 1) + shift)
                n = 1 if b == PLE else 2
                act.activation(w_hi[:, half, 2 * p:2 * p + n, :], w_raw[:, p, 0:n, :], ACT.Copy).then_inc(hi_ready, 1)

            def sums(n, s):
                i = 4 * n + s
                junk = tmp[:, 2 * (s % 2):2 * (s % 2) + 2, :]
                if n == 0:
                    act.wait_ge(x_landed[s], 16)
                    if s >= 2:
                        act.wait_ge(ssq_ready, s - 1)
                else:
                    b = OUT + 3 if n == 1 else LAST - 1
                    act.wait_ge(*emptied(b, s))
                    if s >= 2:
                        wait_filled(act, ("xt", n, s - 2, 1))
                    elif n == 1:
                        for q in range(2):
                            wait_filled(act, ("pt", q))
                    else:
                        act.wait_ge(hid_lo, 4 * NE)
                act.activation(junk.rearrange("p a n -> p (a n)"), h[:, s, :], ACT.Square,
                               accum_out=ssq[:, i:i + 1]).then_inc(ssq_ready, 1)
                act.wait_ge(ssq_ready, i + 1)
                act.activation(rms[:, i:i + 1], ssq[:, i:i + 1], ACT.Sqrt, bias=eps[:], scale=1.0 / D
                               ).then_inc(rms_ready, 1)

            def xt_evac(n, s):
                hi = a_hi if n == 0 else b_hi
                for q in range(2):
                    bank = wait_full(act, ("xt", n, s, q))
                    if n == 2 and s == 0 and q == 0:
                        act.wait_ge(acc_full, 4 * (LAST - 2))
                    act.activation(hi[:, 4 * q:4 * q + 4, s * P:s * P + P],
                                   bank.rearrange("p (k n) -> p k n", k=4), ACT.Copy).then_inc(xt_hi, 1)

            def yt_evac(part, s):
                bank = wait_full(act, ("yt", part, s))
                hi = a_hi if part < 2 else b_hi
                if part == 0:
                    act.wait_ge(acc_full, 4 * (OUT - 1) + s + 1)
                if part == 2 and s == 0:
                    wait_free(act, ("diag", 7))
                q = part % 2
                act.activation(hi[:, 4 * q:4 * q + 4, s * P:s * P + P],
                               bank.rearrange("p (k n) -> p k n", k=4), ACT.Copy).then_inc(yt_hi, 1)

            def relu_evac(b, s, e, trip=0):
                n = 4 * e + s
                act.wait_ge(acc_full, 4 * b + s + 1 + 16 * trip)
                if isinstance(e, int) and n < 2:
                    wait_filled(act, ("xt", 1, 2 + s, 1))
                else:
                    act.wait_ge(sq_ready, n - 1 + 8 * trip)
                act.activation(tmp[:, s % 2, :], acc[:, s, :], ACT.Relu).then_inc(act_evac, 1)

            def hid_evac(s, e, trip=0):
                n = 4 * e + s
                act.wait_ge(sq_ready, n + 1 + 8 * trip)
                act.activation(a_hi[:, 4 * (e % 2) + s, :], tmp[:, 2 + s % 2, :], ACT.Copy).then_inc(hid_hi, 1)

            def exp_seg(j):
                if j:
                    wait_filled(act, ("diag", j - 1))
                act.wait_ge(seg_ready, j + 1)
                act.activation(lm[:], seg[:, j % 2], ACT.Exp).then_inc(exp_done, 1)

            def load_seg(j):
                g, c = divmod(j, 4)
                if j == 0:
                    act.wait_ge(cs_stored, 16)
                if j >= 2:
                    act.wait_ge(exp_done, j - 1)
                row = c * R + g * RG
                act.dma_start(seg[:, j % 2].rearrange("p r n -> p (r n)"),
                              cs_dram[row:row + RG, :].rearrange("r n -> (r n)").partition_broadcast(P)
                              ).then_inc(seg_landed[j % 2], 16)

            act.wait_ge(eps_ready, 1)
            act.activation(early_rms[:], eps[:], ACT.Sqrt).then_inc(sqrt_loaded, 1)
            sums(0, 0)
            split_hi(0, 0)
            xt_evac(0, 0)
            split_hi(0, 1)
            split_hi(0, 2)
            sums(0, 1)
            split_hi(0, 3)
            xt_evac(0, 1)
            sums(0, 2)
            sums(0, 3)

            seg_at = {18: 0, 19: 1}
            seg_at.update({17 + 2 * j: j for j in range(2, 8)})
            for t in range(4 * OUT):
                b, s = divmod(t, 4)
                if 1 <= t < 3:
                    xt_evac(0, t + 1)
                if t >= 22 and t % 2 == 0:
                    exp_seg((t - 20) // 2)
                if t == 17:
                    wait_free(act, "csT")
                    act.dma_start(cs_dram, csT[:]).then_inc(cs_stored, 16)
                if t in seg_at:
                    load_seg(seg_at[t])
                split_hi(b + 1, s)
                if t == 8:
                    act.wait_ge(v_sum, NS)
                    act.activation(v_rms[:], v_ssq[:], ACT.Sqrt, bias=eps[:], scale=1.0 / P).then_inc(v_rms_ready, 1)
                if 10 <= t < 18:
                    bank = wait_full(act, ("xs", t - 10))
                    if t == 10:
                        wait_free(act, ("ws", 1))
                    ins = act.activation(y[:, :, (t - 10) * P:(t - 10) * P + P],
                                         bank.rearrange("p (c n) -> p c n", c=NS), ACT.Copy)
                    freed(ins, ("xs", t - 10))
                if t == 11:
                    bank = wait_full(act, "dt")
                    act.wait_ge(small_landed, 16 * 4)
                    ins = act.activation(dtT[:], bank[0:2 * R, :], ACT.Identity, bias=dt_b[:])
                    freed(ins, "dt")
                if t == 12:
                    act.activation(e_a[:], a_log[:], ACT.Exp).then_inc(ea_ready, 1)
                    act.wait_ge(dt_step, 3)
                    act.activation(dts[:, 2, :], dts[:, 1, :], ACT.Exp).then_inc(dt_exp, 1)
                if t == 16:
                    bank = wait_full(act, "decay")
                    act.wait_ge(cs_ready, 1)
                    ins = act.activation(decay[:].rearrange("p a c r -> p (a c r)"), bank[:, 0:3 * NS * R], ACT.Exp)
                    freed(ins, "decay")
                if 16 <= t < 20:
                    for i in range(2):
                        head = 2 * (t - 16) + i
                        bank = wait_full(act, ("mix", head))
                        ins = act.activation(h[:, :, head * P:head * P + P], bank.rearrange("p (c n) -> p c n", c=NS),
                                             ACT.Identity, bias=cols[:, 60 + head:61 + head])
                        freed(ins, ("mix", head))
                if 19 <= t < 21:
                    g = t - 19
                    bank = wait_full(act, ("b_nat", g))
                    ins = act.activation(b_nat[:, g].rearrange("p c n -> p (c n)"), bank, ACT.Copy)
                    freed(ins, ("b_nat", g))
                if t in (28, 29, 30, 31):
                    i = t - 28
                    act.wait_ge(ya_mul, 4 + i + 1)
                    if i:
                        act.wait_ge(m_ssq_ready, i)
                    act.activation(conv[:].rearrange("p a n -> p (a n)"), h[:, i, :], ACT.Square,
                                   accum_out=m_ssq[:, i:i + 1]).then_inc(m_ssq_ready, 1)
                if t == 31:
                    act.wait_ge(m_ssq_ready, 4)
                    act.activation(m_rms[:, 0:4], m_ssq[:, 0:4], ACT.Sqrt, bias=eps[:], scale=1.0 / W
                                   ).then_inc(m_rms_ready, 1)
                if t == 35:
                    yt_evac(0, 0)
                    yt_evac(0, 1)
                if 32 <= t < 36:
                    i = t - 32
                    act.wait_ge(yb_mul, i + 1)
                    act.wait_ge(m_ssq_ready, 4 + i)
                    act.activation(conv[:, 0, :], y[:, i, 0:512], ACT.Square,
                                   accum_out=m_ssq[:, 4 + i:5 + i]).then_inc(m_ssq_ready, 1)
                if t == 35:
                    act.wait_ge(m_ssq_ready, 8)
                    act.activation(m_rms[:, 4:8], m_ssq[:, 4:8], ACT.Sqrt, bias=eps[:], scale=2.0 / W
                                   ).then_inc(m_rms_ready, 1)
                if t == 19:
                    exp_seg(0)
                act.wait_ge(acc_full, t + 1)
                if b < X:
                    if t < 4:
                        wait_filled(act, ("xt", 0, s, 1))
                    act.activation(h[:, s, 512 * b:512 * b + 512], acc[:, s, :], ACT.Gelu).then_inc(act_evac, 1)
                elif b < U:
                    i = t - 4 * X
                    if i == 0:
                        wait_free(act, "cols")
                    if i >= 2:
                        act.wait_ge(silu_done, i - 1)
                    act.activation(conv[:, i % 2, :], acc[:, s, :], ACT.Copy, scale=cols[:, 36 + i:37 + i]
                                   ).then_inc(conv_begun, 1)
                    act.wait_ge(*emptied(b, s))
                    if i < 8:
                        if i >= 2:
                            wait_filled(act, ("xs", i - 2))
                        dst = xs_t[:, i % 2, :]
                    else:
                        dst = bcT[:, i - 8, :]
                    act.activation(dst, conv[:, i % 2, :], ACT.Silu, bias=cols[:, 48 + i:49 + i]).then_inc(silu_done, 1)
                elif b < Z:
                    i = t - 4 * U
                    if i < 4:
                        act.wait_ge(v_sum, NS)
                    else:
                        act.wait_ge(ya_mul, i - 3)
                    act.activation(tmp[:, s, :], acc[:, s, :], ACT.Gelu).then_inc(act_evac, 1)
                else:
                    i = t - 4 * Z
                    act.wait_ge(ya_mul, 5 + i) if i < 4 else act.wait_ge(yb_mul, i - 3)
                    act.activation(tmp[:, s, :], acc[:, s, :], ACT.Silu).then_inc(act_evac, 1)

            for i in range(4):
                act.wait_ge(yb_mul, 4 + i + 1)
                act.wait_ge(m_ssq_ready, 8 + i)
                act.activation(conv[:, 0, :], y[:, i, 512:1024], ACT.Square,
                               accum_out=m_ssq[:, 8 + i:9 + i]).then_inc(m_ssq_ready, 1)
            act.wait_ge(m_ssq_ready, 12)
            act.activation(m_rms[:, 8:12], m_ssq[:, 8:12], ACT.Sqrt, bias=eps[:], scale=2.0 / W
                           ).then_inc(m_rms_ready, 1)
            yt_evac(0, 2)
            yt_evac(0, 3)
            for b in range(OUT, OUT + 4):
                for s in range(4):
                    split_hi(b + 1, s)
                    t = 4 * b + s
                    if b == OUT and s < 2:
                        for i in (2 * s, 2 * s + 1):
                            yt_evac(1, i)
                    if 41 <= t < 45:
                        for q in range(2):
                            yt_evac(2 + q, t - 41)
                    if t == 45:
                        for k in range(2):
                            bank = wait_full(act, ("pt", k))
                            act.activation(p_hi[:, k, :], bank, ACT.Copy).then_inc(pt_hi, 1)
                    if b == OUT + 3:
                        if s >= 2:
                            xt_evac(1, s - 2)
                        sums(1, s)

            for s in range(4):
                split_hi(FF, s)
                if s == 0:
                    xt_evac(1, 2)
                if s == 2:
                    xt_evac(1, 3)
                act.wait_ge(acc_full, 4 * PLE + s + 1)
                if s == 0:
                    for i in range(NS):
                        wait_filled(act, ("yt", 3, i))
                i = 2 * (s % 2)
                act.activation(y[:, s, :].rearrange("p (a n) -> p a n", a=2), acc[:, i:i + 2, :],
                               ACT.Copy).then_inc(act_evac, 1)

            def ff1(b, e, trip=0):
                for s in range(4):
                    split_hi(b + 1, s, 16 * trip, trip=trip)
                    relu_evac(b, s, e, trip)
                    hid_evac(s, e, trip)

            def ff2(b, trip=0):
                for s in range(4):
                    split_hi(b + 1, s, 16 * trip, trip=trip)

            ff1(FF, 0)
            with act.Fori(0, 3) as i:
                for q in range(2):
                    ff1(FF + 1 + 2 * q, 1 + q, i)
                    ff2(FF + 2 + 2 * q, i)
            ff1(LAST - 3, 7)
            ff2(LAST - 2)
            for s in range(4):
                split_hi(GATE, s)
                if s >= 2:
                    xt_evac(2, s - 2)
                sums(2, s)

            for i in range(8):
                b, s = GATE + i // 4, i % 4
                if i == 0:
                    xt_evac(2, 2)
                if i == 2:
                    xt_evac(2, 3)
                if b == GATE:
                    split_hi(GATE + 1, s)
                act.wait_ge(acc_full, 4 * b + s + 1)
                if i >= 2:
                    act.wait_ge(gated, i - 1)
                act.activation(conv[:, i % 2, :], acc[:, s, :], ACT.Sigmoid).then_inc(act_evac, 1)
                if b > GATE:
                    act.wait_ge(sqrt_loaded, s + 1)
                    act.activation(early_rms[:], eps[:], ACT.Sqrt).then_inc(sqrt_loaded, 1)
                act.wait_ge(h_final, i + 1)
                if i:
                    act.wait_ge(f_ssq_ready, i)
                act.activation(xs_t[:, 0, :], h[:, s, 512 * (i // 4):512 * (i // 4) + 512], ACT.Square,
                               accum_out=f_ssq[:, i:i + 1]).then_inc(f_ssq_ready, 1)
                act.wait_ge(f_ssq_ready, i + 1)
                if b == GATE:
                    act.activation(f_base[:, s:s + 1], f_ssq[:, i:i + 1], ACT.Identity, bias=eps[:], scale=1.0 / D
                                   ).then_inc(f_base_ready, 1)
                else:
                    act.wait_ge(f_base_ready, s + 1)
                    act.activation(f_rms[:, s:s + 1], f_ssq[:, i:i + 1], ACT.Sqrt, bias=f_base[:, s:s + 1],
                                   scale=1.0 / D).then_inc(f_rms_ready, 1)
                if i == 7:
                    act.wait_ge(f_rstd_ready, s + 1)
                    act.wait_ge(h_gain, 4 + s + 1)
                    act.activation(y[:, s, OUT_DVE:], y[:, s, OUT_DVE:], ACT.Copy, scale=f_rstd[:, s:s + 1]
                                   ).then_inc(out_act, 1)

        @block.vector
        def _(dve):
            def split_lo(b, p, trip=0):
                half = b % 2
                dve.wait_ge(hi_ready, 4 * b + p + 1 + 16 * trip)
                n = 1 if b == PLE else 2
                dve.tensor_tensor(w_lo[:, half, 2 * p:2 * p + n, :], w_raw[:, p, 0:n, :],
                                  w_hi[:, half, 2 * p:2 * p + n, :].bitcast(F32), ALU.subtract).then_inc(lo_ready, 1)

            def normed(n, s):
                i = 4 * n + s
                dve.wait_ge(rms_ready, i + 1)
                dve.reciprocal(rstd[:, i:i + 1], rms[:, i:i + 1]).then_inc(rstd_ready, 1)
                dve.wait_ge(rstd_ready, i + 1)
                slot, use = ((0, 1), (0, 3), (1, 3))[n]
                if s == 0:
                    dve.wait_ge(gain_landed[slot], 16 * use)
                if n == 0:
                    dst = h[:, s, :]
                else:
                    dst = tmp[:, 2 * (s % 2):2 * (s % 2) + 2, :].rearrange("p a n -> p (a n)")
                dve.scalar_tensor_tensor(dst, h[:, s, :], rstd[:, i:i + 1], gain[:, slot, :], ALU.mult, ALU.mult
                                         ).then_inc(xn_ready, 1)

            def xt_evac(n, s):
                hi, lo = (a_hi, a_lo) if n == 0 else (b_hi, b_lo)
                for q in range(2):
                    name = ("xt", n, s, q)
                    bank = side[:, fills[name][0], :]
                    dve.wait_ge(xt_hi, 8 * n + 2 * s + q + 1)
                    at = (slice(None), slice(4 * q, 4 * q + 4), slice(s * P, s * P + P))
                    dve.tensor_tensor(lo[at], bank.rearrange("p (k n) -> p k n", k=4), hi[at].bitcast(F32),
                                      ALU.subtract).then_inc(side_free[fills[name][0]], 1)

            def yt_evac(part, s, n):
                name = ("yt", part, s)
                bank = side[:, fills[name][0], :]
                hi, lo = (a_hi, a_lo) if part < 2 else (b_hi, b_lo)
                q = part % 2
                dve.wait_ge(yt_hi, n + 1)
                at = (slice(None), slice(4 * q, 4 * q + 4), slice(s * P, s * P + P))
                dve.tensor_tensor(lo[at], bank.rearrange("p (k n) -> p k n", k=4), hi[at].bitcast(F32),
                                  ALU.subtract).then_inc(side_free[fills[name][0]], 1)

            def add_group(b, s, base=None, trip=0):
                dve.wait_ge(acc_full, 4 * b + s + 1 + 16 * trip)
                if b == OUT:
                    dve.wait_ge(x_landed[s], 32)
                else:
                    prev = before[b] + s + 1 - 4
                    dve.wait_ge(dve_evac, prev + 8 * trip)
                i = 2 * (s % 2)
                hs = h[:, s, :].rearrange("p (a n) -> p a n", a=2)
                dve.tensor_tensor(hs, hs, acc[:, i:i + 2, :], ALU.add).then_inc(dve_evac, 1)

            dve.memset(eps[:], EPS).then_inc(eps_ready, 1)
            normed(0, 0)
            split_lo(0, 0)
            xt_evac(0, 0)
            split_lo(0, 1)
            split_lo(0, 2)
            normed(0, 1)
            split_lo(0, 3)
            xt_evac(0, 1)
            normed(0, 2)
            normed(0, 3)

            step = [0]

            def chain(ins):
                step[0] += 1
                ins.then_inc(dt_step, 1)
                dve.wait_ge(dt_step, step[0])

            done = [0]

            d = [dts[:, i, :] for i in range(5)]

            def ssd(ins):
                done[0] += 1
                ins.then_inc(ssd_step, 1)
                dve.wait_ge(ssd_step, done[0])

            def mask_cb(j):
                bank = wait_full(dve, ("cb", j))
                if j:
                    dve.wait_ge(lm_ready, j)
                ins = dve.tensor_tensor(cbm[:], bank[:, 0:P], upper[:], ALU.mult)
                freed(ins, ("cb", j))
                wait_free(dve, ("cb", j))
                dve.wait_ge(exp_done, j + 1)
                dve.tensor_tensor(lm[:], lm[:], cbm[:, None, :].broadcast_to([P, RG, P]), ALU.mult
                                  ).then_inc(lm_ready, 1)

            for t in range(4 * OUT):
                b, s = divmod(t, 4)
                if 1 <= t < 3:
                    xt_evac(0, t + 1)
                if t == 16:
                    bank = wait_full(dve, "decay")
                    dve.tensor_copy(cs[:], bank[:, 0:NS * R]).then_inc(cs_ready, 1)
                if t == 17:
                    bank = wait_full(dve, "csT")
                    freed(dve.tensor_copy(csT[:], bank[0:NS * R, 0:P]), "csT")
                if t >= 22 and t % 2 == 0:
                    mask_cb((t - 20) // 2)
                split_lo(b + 1, s)
                if t == 3:
                    bank = wait_full(dve, "cols")
                    freed(dve.tensor_copy(cols[:], bank[:, 0:68]), "cols")
                if t == 4:
                    dve.wait_ge(small_landed, 16 * 4)
                    dve.wait_ge(wdt_zero, 2)
                    dve.tensor_copy(wdt_hl[:, :, 0:R], w_dt[:]).then_inc(wdt_ready, 1)
                    dve.tensor_copy(wdt_h[:, :, 0:R], w_dt[:]).then_inc(wdt_ready, 1)
                    dve.wait_ge(wdt_ready, 1)
                    dve.tensor_tensor(wdt_hl[:, :, R:2 * R], w_dt[:], wdt_hl[:, :, 0:R].bitcast(F32), ALU.subtract
                                      ).then_inc(wdt_ready, 1)
                if t == 5:
                    for i in range(2):
                        bank = wait_full(dve, ("ws", i))
                        up = upper[:, None, :].broadcast_to([P, 4, P])
                        freed(dve.tensor_tensor(wsT[:, 4 * i:4 * i + 4, :], bank.rearrange("p (g n) -> p g n", g=4),
                                                up, ALU.mult), ("ws", i))
                if 5 <= t < 9:
                    i = t - 5
                    dve.wait_ge(v_sq, i + 1)
                    dve.tensor_reduce(v_ssq[:, i, :], tmp[:, 2 * (i % 2):2 * (i % 2) + 2, :].rearrange(
                        "p a (g n) -> p (a g) n", n=P), AX.X, ALU.add).then_inc(v_sum, 1)
                if t == 9:
                    dve.wait_ge(v_rms_ready, 1)
                    dve.reciprocal(v_rstd[:], v_rms[:]).then_inc(v_rstd_ready, 1)
                    dve.wait_ge(v_rstd_ready, 1)
                if t == 12:
                    bank = wait_full(dve, "dt_nat")
                    dn = bank[:, 0:2 * NS * R].rearrange("p (c k r) -> p c k r", c=NS, k=2)
                    d0 = d[0].rearrange("p (c r) -> p c r", c=NS)
                    chain(dve.tensor_copy(d0, dn[:, :, 0, :]))
                    ins = dve.tensor_tensor(d0, dn[:, :, 1, :], d0, ALU.add)
                    freed(ins, "dt_nat")
                    wait_free(dve, "dt_nat")
                    chain(dve.tensor_scalar(d[4], d[0], 0.0, None, ALU.max))
                    chain(dve.scalar_tensor_tensor(d[1], d[0], -1.0, d[0], ALU.mult, ALU.min))
                if t >= 21 and t % 2 == 1:
                    j = (t - 21) // 2
                    g, c = divmod(j, 4)
                    yv = y[:, c, 512 * g:512 * g + 512]
                    term = xs_t[:, 0, :]
                    heads = slice(g * RG, g * RG + RG)
                    diag = wait_full(dve, ("diag", j))
                    dve.wait_ge(xsd_ready, j + 1)
                    if c:
                        off = wait_full(dve, ("off", j))
                        ins = dve.tensor_tensor(
                            term.rearrange("p (r d) -> p r d", r=RG), off.rearrange("p (r d) -> p r d", r=RG),
                            decay[:, 0, c, heads][:, :, None].broadcast_to([P, RG, HD]), ALU.mult)
                        freed(ins, ("off", j))
                        wait_free(dve, ("off", j))
                        ssd(dve.tensor_tensor(term, term, yv, ALU.add))
                        ins = dve.tensor_tensor(yv, diag, term, ALU.add)
                    else:
                        ins = dve.tensor_tensor(yv, diag, yv, ALU.add)
                    freed(ins, ("diag", j))
                    if c < 3:
                        new = wait_full(dve, ("state", j))
                        if c:
                            cv = carry[:].rearrange("p (r d) -> p r d", r=RG)
                            ssd(dve.tensor_tensor(cv, cv, decay[:, 2, c, heads][:, :, None].broadcast_to([P, RG, HD]),
                                                  ALU.mult))
                            ins = dve.tensor_tensor(carry[:], new, carry[:], ALU.add)
                        else:
                            ins = dve.tensor_copy(carry[:], new)
                        freed(ins, ("state", j))
                        wait_free(dve, ("state", j))
                if t == 35:
                    yt_evac(0, 0, 0)
                    yt_evac(0, 1, 1)
                if t == 32:
                    dve.wait_ge(m_rms_ready, 1)
                    dve.reciprocal(m_rstd[:, 0:4], m_rms[:, 0:4]).then_inc(m_rstd_ready, 1)
                    dve.wait_ge(m_rstd_ready, 1)
                    dve.wait_ge(gain_landed[0], 32)
                    for i in range(NS):
                        dve.scalar_tensor_tensor(h[:, i, :], h[:, i, :], m_rstd[:, i:i + 1], gain[:, 0, :],
                                                 ALU.mult, ALU.mult).then_inc(ya_norm, 1)
                if t == 19:
                    mask_cb(0)
                if X <= b < U:
                    i = t - 4 * X
                    dve.wait_ge(conv_begun, i + 1)
                    for k in range(1, 4):
                        w = cols[:, 12 * (3 - k) + i:12 * (3 - k) + i + 1]
                        dst = conv[:, i % 2, k:SEQ]
                        ins = dve.scalar_tensor_tensor(dst, acc[:, s, 0:SEQ - k], w, dst, ALU.mult, ALU.add)
                        if k < 3:
                            ins.then_inc(conv_step, 1)
                            dve.wait_ge(conv_step, 2 * i + k)
                        else:
                            ins.then_inc(dve_evac, 1)
                    if t == 13:
                        dve.wait_ge(dt_exp, 1)
                        chain(dve.tensor_scalar(d[0], d[2], 2.0, None, ALU.add))
                        chain(dve.reciprocal(d[1], d[0]))
                        chain(dve.tensor_tensor(d[2], d[2], d[1], ALU.mult))
                        chain(dve.tensor_tensor(d[0], d[2], d[2], ALU.mult))
                        chain(dve.tensor_scalar(d[1], d[0], 1.0 / 17, None, ALU.mult))
                        for m in (15, 13, 11):
                            chain(dve.scalar_tensor_tensor(d[1], d[1], 1.0 / m, d[0], ALU.add, ALU.mult))
                    if t == 14:
                        for m in (9, 7, 5, 3):
                            chain(dve.scalar_tensor_tensor(d[1], d[1], 1.0 / m, d[0], ALU.add, ALU.mult))
                        chain(dve.scalar_tensor_tensor(d[1], d[1], 1.0, d[2], ALU.add, ALU.mult))
                        dtf = dt[:].rearrange("p c r -> p (c r)")
                        dve.scalar_tensor_tensor(dtf, d[1], 2.0, d[4], ALU.mult, ALU.add).then_inc(dt_ready, 1)
                        dve.wait_ge(dt_ready, 1)
                        dve.wait_ge(ea_ready, 1)
                        ea = e_a[:, None, :].broadcast_to([P, NS, R])
                        dve.scalar_tensor_tensor(dA[:], dt[:], -1.0, ea, ALU.mult, ALU.mult).then_inc(dA_ready, 1)
                    if 9 <= t < 13:
                        hv = h[:, t - 9, :].rearrange("p (g n) -> p g n", g=GH)
                        dve.tensor_tensor(hv, hv, v_rstd[:, t - 9, :][:, :, None].broadcast_to([P, GH, P]),
                                          ALU.mult).then_inc(v_scaled, 1)
                elif U <= b < Z:
                    i = t - 4 * U
                    dve.wait_ge(*emptied(b, s))
                    if i == 0 or i == 4:
                        for head in range(4 * (i // 4), 4 * (i // 4) + 4):
                            wait_free(dve, ("mix", head))
                    c0 = 512 * (b - U)
                    hv = h[:, s, c0:c0 + 512]
                    dve.tensor_tensor(hv, hv, tmp[:, s, :], ALU.mult).then_inc(ya_mul, 1)
                elif b >= Z:
                    g = b - Z
                    dve.wait_ge(*emptied(b, s))
                    wait_free(dve, ("diag", 4 * g + s))
                    yv = y[:, s, 512 * g:512 * g + 512]
                    dve.tensor_tensor(yv, yv, tmp[:, s, :], ALU.mult).then_inc(yb_mul, 1)

            def yb_scale(g):
                at = slice(4 + 4 * g, 8 + 4 * g)
                dve.wait_ge(m_rms_ready, 2 + g)
                dve.reciprocal(m_rstd[:, at], m_rms[:, at]).then_inc(m_rstd_ready, 1)
                dve.wait_ge(m_rstd_ready, 2 + g)
                dve.wait_ge(gain_landed[1], 32)
                for i in range(NS):
                    yv = y[:, i, 512 * g:512 * g + 512]
                    dve.scalar_tensor_tensor(yv, yv, m_rstd[:, 4 + 4 * g + i:5 + 4 * g + i],
                                             gain[:, 1, 512 * g:512 * g + 512], ALU.mult, ALU.mult).then_inc(yb_norm, 1)

            yt_evac(0, 2, 2)
            yt_evac(0, 3, 3)
            for b in range(OUT, OUT + 4):
                for s in range(4):
                    t = 4 * b + s
                    split_lo(b + 1, s)
                    if b == OUT and s < 2:
                        for i in (2 * s, 2 * s + 1):
                            yt_evac(1, i, 4 + i)
                    if 41 <= t < 45:
                        for q in range(2):
                            yt_evac(2 + q, t - 41, 8 + 2 * (t - 41) + q)
                    if t == 45:
                        for k in range(2):
                            dve.wait_ge(pt_hi, k + 1)
                            name = ("pt", k)
                            dve.tensor_tensor(p_lo[:, k, :], side[:, fills[name][0], :], p_hi[:, k, :].bitcast(F32),
                                              ALU.subtract).then_inc(side_free[fills[name][0]], 1)
                    if b == OUT + 3 and s >= 2:
                        xt_evac(1, s - 2)
                    add_group(b, s)
                    if b == OUT and s % 2:
                        yb_scale(s // 2)
                    if b == OUT + 3:
                        normed(1, s)

            for s in range(4):
                split_lo(FF, s)
                if s == 0:
                    xt_evac(1, 2)
                if s == 2:
                    xt_evac(1, 3)

            def ff1(b, e, trip=0):
                for s in range(4):
                    n = 4 * e + s
                    split_lo(b + 1, s, trip=trip)
                    dve.wait_ge(act_evac, before[b] + s + 1 + 8 * trip)
                    if not (isinstance(e, int) and n < 2) or not isinstance(trip, int):
                        dve.wait_ge(hid_lo, n - 1 + 8 * trip)
                    dve.tensor_tensor(tmp[:, 2 + s % 2, :], tmp[:, s % 2, :], tmp[:, s % 2, :], ALU.mult
                                      ).then_inc(sq_ready, 1)
                    dve.wait_ge(hid_hi, n + 1 + 8 * trip)
                    k = 4 * (e % 2) + s
                    dve.tensor_tensor(a_lo[:, k, :], tmp[:, 2 + s % 2, :], a_hi[:, k, :].bitcast(F32), ALU.subtract
                                      ).then_inc(hid_lo, 1)

            def ff2(b, trip=0):
                for s in range(4):
                    split_lo(b + 1, s, trip=trip)
                    add_group(b, s, trip=trip)

            ff1(FF, 0)
            with dve.Fori(0, 3) as i:
                for q in range(2):
                    ff1(FF + 1 + 2 * q, 1 + q, i)
                    ff2(FF + 2 + 2 * q, i)
            ff1(LAST - 3, 7)
            ff2(LAST - 2)
            for s in range(4):
                split_lo(GATE, s)
                if s >= 2:
                    xt_evac(2, s - 2)
                add_group(LAST - 1, s)
                normed(2, s)

            for i in range(8):
                b, s = GATE + i // 4, i % 4
                if i == 0:
                    xt_evac(2, 2)
                if i == 2:
                    xt_evac(2, 3)
                if b == GATE:
                    split_lo(GATE + 1, s)
                at = slice(512 * (i // 4), 512 * (i // 4) + 512)
                dve.wait_ge(*emptied(b, s))
                dve.tensor_tensor(y[:, s, at], y[:, s, at], conv[:, i % 2, :], ALU.mult).then_inc(gated, 1)
                dve.wait_ge(gated, i + 1)
                dve.tensor_tensor(h[:, s, at], h[:, s, at], y[:, s, at], ALU.add).then_inc(h_final, 1)
                dve.wait_ge(h_final, i + 1)
                if i == 0:
                    dve.wait_ge(gain_landed[0], 16 * 4)
                dve.tensor_tensor(y[:, s, at], h[:, s, at], gain[:, 0, at], ALU.mult).then_inc(h_gain, 1)
                if b > GATE:
                    dve.wait_ge(f_rms_ready, s + 1)
                    dve.reciprocal(f_rstd[:, s:s + 1], f_rms[:, s:s + 1]).then_inc(f_rstd_ready, 1)
                    dve.wait_ge(f_rstd_ready, s + 1)
                    dve.wait_ge(h_gain, i + 1)
                    end = OUT_DVE if i == 7 else D
                    dve.tensor_scalar(y[:, s, 0:end], y[:, s, 0:end], f_rstd[:, s:s + 1], None, ALU.mult
                                      ).then_inc(out_dve, 1)

        @block.tensor
        def _(pe):
            def banks_free(b, s, trip=None):
                if b == 0:
                    return
                c, r = last_user(b, s)
                signal, value = emptied(c, r)
                pe.wait_ge(signal, value if trip is None else value + 8 * trip)
                if trip is not None and b == FF + 1:
                    signal, value = emptied(FF + 4, 2 + s // 2)
                    pe.wait_ge(signal, value - 8 + 8 * trip)

            def split_ready(b, p, trip=0):
                pe.wait_ge(lo_ready, 4 * b + p + 1 + 16 * trip)

            def product(dst, st, mv, start, stop):
                pe.matmul(dst, st[0], mv[0], start=start, stop=False)
                pe.matmul(dst, st[0], mv[1], start=False, stop=False)
                return pe.matmul(dst, st[1], mv[0], start=False, stop=stop)

            def group_rows(b, s, act_hl, between=None):
                banks_free(b, s)
                for k in range(KT):
                    if between and k == KT - 2:
                        between()
                    if b == 0 and k % 4 == 0:
                        wait_free(pe, ("xt", 0, s, k // 4))
                    if s == 0 and k % 2 == 0:
                        split_ready(b, k // 2)
                    at = (slice(None), k, slice(s * P, s * P + P))
                    ins = product(acc[:, s, :], [t[at] for t in act_hl],
                                  [t[:, b % 2, k, :] for t in (w_hi, w_lo)], k == 0, k == KT - 1)
                ins.then_inc(acc_full, 1)

            def group_cols(b, s, act_hl, trip=None):
                banks_free(b, s, trip)
                for k in range(KT):
                    if s == 0 and k % 2 == 0:
                        split_ready(b, k // 2, 0 if trip is None else trip)
                    ins = product(acc[:, s, :], [t[:, b % 2, k, s * P:s * P + P] for t in (w_hi, w_lo)],
                                  [t[:, k, :] for t in act_hl], k == 0, k == KT - 1)
                ins.then_inc(acc_full, 1)

            def group_pair(b, s, act_hl, k0, trip=None, nk=4, between=None):
                banks_free(b, s, trip)
                for n in range(2):
                    if between and n == 1:
                        between()
                    for k in range(nk):
                        if s == 0 and n == 0 and nk == 4:
                            split_ready(b, k, 0 if trip is None else trip)
                        elif s == 0 and nk == 2:
                            split_ready(b, 2 * k + n)
                        sub = 2 * k + n if nk == 4 else 2 * (2 * k + n)
                        at = (slice(None), k0 + k, slice(s * P, s * P + P))
                        ins = product(acc[:, 2 * (s % 2) + n, :], [t[at] for t in act_hl],
                                      [t[:, b % 2, sub, :] for t in (w_hi, w_lo)], k == 0, k == nk - 1)
                ins.then_inc(acc_full, 1)

            def open_bank(name):
                bank, n = fills[name]
                if n:
                    pe.wait_ge(side_free[bank], n)
                return side[:, bank, :]

            def filled(ins, name):
                ins.then_inc(side_full[fills[name][0]], 1)

            def turn(name, src):
                bank = open_bank(name)
                for i in range(4):
                    ins = pe.transpose(bank[:, i * P:i * P + P], src(i), ident[:])
                filled(ins, name)

            def turn_norm(n, s):
                pe.wait_ge(xn_ready, 4 * n + s + 1)
                src = h[:, s, :] if n == 0 else tmp[:, 2 * (s % 2):2 * (s % 2) + 2, :].rearrange("p a n -> p (a n)")
                for q in range(2):
                    turn(("xt", n, s, q), lambda i: src[:, (4 * q + i) * P:(4 * q + i + 1) * P])

            A, B = (a_hi, a_lo), (b_hi, b_lo)

            pe.wait_ge(consts_ready, 3)
            for i in range(WARM):
                pe.matmul(acc[:, i % 2, 0:P], ident[:], ones[:], start=True, stop=True)
            turn_norm(0, 0)
            for i in range(WARM):
                pe.matmul(acc[:, i % 2, 0:P], ident[:], ones[:], start=True, stop=True)

            for t in range(4 * OUT):
                b, s = divmod(t, 4)
                if X <= b < U:
                    group_cols(b, s, A)
                else:
                    group_rows(b, s, A, (lambda: turn_norm(0, t + 1)) if t < NS - 1 else None)
                if t == 2:
                    pe.wait_ge(rows_landed, 16 * 3)
                    filled(pe.transpose(open_bank("cols")[:, 0:68], rows[0:68, :], ident[0:68, 0:68]), "cols")
                if t == 4:
                    pe.wait_ge(ws_landed, 16)
                    for i in range(2):
                        turn(("ws", i), lambda g: y[:, 0, (4 * i + g) * P:(4 * i + g + 1) * P])
                if 9 <= t < 17:
                    i = t - 9
                    pe.wait_ge(silu_done, i + 1)
                    turn(("xs", i), lambda c: xs_t[:, i % 2, c * P:c * P + P])
                if t == 10:
                    bank = open_bank("dt")
                    pe.wait_ge(wdt_ready, 3)
                    for k in range(KT):
                        pe.matmul(bank, wdt_hl[:, k, :], a_hi[:, k, :], start=(k == 0), stop=False)
                        ins = pe.matmul(bank, wdt_h[:, k, :], a_lo[:, k, :], start=False, stop=(k == KT - 1))
                    filled(ins, "dt")
                if t == 11:
                    bank = open_bank("dt_nat")
                    wait_free(pe, "dt")
                    for c in range(NS):
                        ins = pe.transpose(bank[:, 2 * c * R:2 * (c + 1) * R], dtT[:, c * P:c * P + P],
                                           ident[0:2 * R, 0:2 * R])
                    filled(ins, "dt_nat")
                if t == 16:
                    pe.wait_ge(cs_ready, 1)
                    filled(pe.transpose(open_bank("csT")[0:NS * R, 0:P], cs[:], ident[:]), "csT")
                if 15 <= t < 19:
                    if t == 15:
                        pe.wait_ge(v_ready, NS)
                        wait_free(pe, ("ws", 1))
                    for i in range(2):
                        g = 2 * (t - 15) + i
                        bank = open_bank(("mix", g))
                        filled(pe.matmul(bank.rearrange("p (c n) -> p c n", c=NS), wsT[:, g, :],
                                         h[:, :, g * P:g * P + P], start=True, stop=True), ("mix", g))
                if t == 15:
                    bank = open_bank("decay")
                    pe.wait_ge(dA_ready, 1)
                    for i, m in enumerate((upper, after, ones)):
                        ins = pe.matmul(bank[:, i * NS * R:(i + 1) * NS * R], m[:],
                                        dA[:].rearrange("p c r -> p (c r)"), start=True, stop=True)
                    filled(ins, "decay")
                if 18 <= t < 20:
                    g = t - 18
                    pe.wait_ge(silu_done, 9 + g)
                    turn(("b_nat", g), lambda c: bcT[:, g, c * P:c * P + P])
                if t >= 19 and t % 2 == 1 and t < 35:
                    j = (t - 19) // 2
                    g, c = divmod(j, 4)
                    at = slice(c * P, c * P + P)
                    bank = open_bank(("cb", j))
                    if j % 4 == 0:
                        pe.wait_ge(silu_done, 11 + g)
                    filled(pe.matmul(bank[:, 0:P], bcT[:, g, at], bcT[:, 2 + g, at], start=True, stop=True), ("cb", j))
                if t >= 20 and t % 2 == 0:
                    j = (t - 20) // 2
                    g, c = divmod(j, 4)
                    at = slice(c * P, c * P + P)
                    if c:
                        bank = open_bank(("off", j))
                        wait_free(pe, ("state", j - 1))
                        filled(pe.matmul(bank, bcT[:, 2 + g, at], carry[:], start=True, stop=True), ("off", j))
                    pe.wait_ge(xdt_ready, 2 * j + 2)
                    bank = open_bank(("diag", j))
                    pe.wait_ge(lm_ready, j + 1)
                    for r in range(RG):
                        ins = pe.matmul(bank[:, r * HD:r * HD + HD], lm[:, r, :], xdt[:, r * HD:r * HD + HD],
                                        start=True, stop=True)
                    filled(ins, ("diag", j))
                    if c < 3:
                        bank = open_bank(("state", j))
                        if c == 0:
                            wait_free(pe, ("b_nat", g))
                        filled(pe.matmul(bank, b_nat[:, g, c, :], xdd[:], start=True, stop=True), ("state", j))

                if t >= 34:
                    if t == 34:
                        pe.wait_ge(ya_norm, NS)
                    for k in (2 * (t - 34), 2 * (t - 34) + 1):
                        turn(("yt", 0, k), lambda i: h[:, k, i * P:i * P + P])

            for b in range(OUT, OUT + 4):
                for s in range(4):
                    t = 4 * b + s
                    if b < OUT + 2:
                        wait_free(pe, ("yt", b - OUT, s))
                    elif b == OUT + 2:
                        for q in range(2):
                            wait_free(pe, ("yt", 2 + q, s))
                    def second_half(tiles):
                        for i in tiles:
                            turn(("yt", 1, i), lambda k: h[:, i, (4 + k) * P:(5 + k) * P])

                    group_pair(b, s, A if b < OUT + 2 else B, 4 * ((b - OUT) % 2),
                               between=(lambda: second_half((0, 1))) if t == 4 * OUT else None)
                    if t == 4 * OUT:
                        second_half((2, 3))
                    if 40 <= t < 44:
                        i = t - 40
                        pe.wait_ge(yb_norm, 5 + i)
                        for q in range(2):
                            turn(("yt", 2 + q, i), lambda k: y[:, i, (4 * q + k) * P:(4 * q + k + 1) * P])
                    if t == 44:
                        pe.wait_ge(p_landed, 16)
                        for q in range(2):
                            turn(("pt", q), lambda i: tmp[:, i // 2, 256 * (i % 2) + q * P:256 * (i % 2) + (q + 1) * P])
                    if b == OUT + 3 and s:
                        turn_norm(1, s - 1)

            for k in range(2):
                wait_free(pe, ("pt", k))
            for s in range(4):
                group_pair(PLE, s, (p_hi, p_lo), 0, nk=2)
                if s == 1:
                    turn_norm(1, 3)

            def ff1(b, trip=None):
                for s in range(4):
                    group_cols(b, s, B, trip)

            def ff2(b, e, trip=None):
                for s in range(4):
                    if s == 0:
                        pe.wait_ge(hid_lo, 4 * e + 4 + (0 if trip is None else 8 * trip))
                    group_pair(b, s, A, 4 * (e % 2), trip)

            for s in range(NS):
                for q in range(2):
                    wait_free(pe, ("xt", 1, s, q))
            ff1(FF)
            with pe.Fori(0, 3) as i:
                for q in range(2):
                    ff1(FF + 1 + 2 * q, i)
                    ff2(FF + 2 + 2 * q, q, i)
            ff1(LAST - 3)
            ff2(LAST - 2, 6)
            for s in range(4):
                if s == 0:
                    pe.wait_ge(hid_lo, 4 * NE)
                group_pair(LAST - 1, s, A, 4)
                if s:
                    turn_norm(2, s - 1)

            for i in range(8):
                b, s = GATE + i // 4, i % 4
                if b == GATE:
                    for q in range(2):
                        wait_free(pe, ("xt", 2, s, q))
                group_rows(b, s, B)
                if i == 1:
                    turn_norm(2, 3)


_INS = ["x", "p", "norm_mix_g", "w_in", "gm_v_norm_g", "gm_ws", "gm_bs", "gm_out_norm_g", "ssd_conv_w", "ssd_conv_b",
        "ssd_dt_bias", "ssd_a_log", "ssd_d", "ssd_norm_g", "w_out", "norm_mlp_g", "w_ff1", "w_ff2", "ple_norm_g",
        "w_ple_gate", "w_ple_proj", "final_norm_g"]


def kernel(**inputs):
    import numpy as np
    import concourse.bacc as bacc
    from concourse.bass_utils import run_bass_kernel_spmd

    nc = bacc.Bacc("TRN2", target_bir_lowering=False, num_devices=1)
    arrays, aps = {}, {}
    for name in _INS:
        arr = np.ascontiguousarray(inputs[name])
        arrays[f"in_{name}"] = arr
        aps[name] = nc.dram_tensor(f"in_{name}", arr.shape, mybir.dt.from_np(arr.dtype), kind="ExternalInput").ap()
    shape = inputs["x"].shape
    out = nc.dram_tensor("out_0", shape, F32, kind="ExternalOutput").ap()
    build_layer(nc, aps, out)
    r = run_bass_kernel_spmd(nc, [arrays], core_ids=[0])
    return r.results[0]["out_0"]
```
